# Optimizing a Trainium2 kernel written in Bass

```python
import jax, jax.numpy as jnp
from jax import lax
import numpy as np

D_MODEL = 2048
BATCH = 1
SEQ = 256
DEPTH = 2

GRID_W = 64
CTX_LEN = 256
N_MIXERS = 2
N_POOL_LAYERS = (DEPTH + 1) // 2
N_MLA_LAYERS = DEPTH // 2
POOL_WINDOWS = (2, 4, 8, 16)
POOL_GROUPS = len(POOL_WINDOWS)
POOL_GW = D_MODEL // POOL_GROUPS
N_HEADS = 16
Q_LORA = 512
KV_LORA = 512
QK_NOPE = 128
ROPE_DIM = 64
AXIS_DIM = ROPE_DIM // 2
V_DIM = 128
QK_DIM = QK_NOPE + ROPE_DIM
ATTN_SCALE = QK_DIM ** -0.5
ROPE_BASE = 10000.0
Q_BLOCK = 128
D_FF = ((8 * D_MODEL // 3 + 255) // 256) * 256
RMS_EPS = 1e-6
N_MOD = 6

kernel_name = "interleaved_pool_mla_prefix_dit"

def rmsnorm(x, g):
    xf = x.astype(jnp.float32)
    xf = xf * lax.rsqrt(jnp.mean(xf * xf, axis=-1, keepdims=True) + RMS_EPS)
    return (xf * g.astype(jnp.float32)).astype(x.dtype)

def modulate(h, shift, scale):
    return h * (1.0 + scale) + shift

def swiglu(u, w1, w3, w2):
    return (jax.nn.silu(u @ w1) * (u @ w3)) @ w2

def axial_rope_tables(L):
    rows = L // GRID_W
    row = jnp.repeat(jnp.arange(rows, dtype=jnp.float32), GRID_W)
    col = jnp.tile(jnp.arange(GRID_W, dtype=jnp.float32), rows)
    inv = ROPE_BASE ** (-jnp.arange(0, AXIS_DIM, 2, dtype=jnp.float32) / AXIS_DIM)
    ang = jnp.stack([row[:, None] * inv, col[:, None] * inv], axis=1)
    return jnp.cos(ang), jnp.sin(ang)

def apply_axial_rope(x, cos, sin):
    extra = x.ndim - 3
    half = AXIS_DIM // 2
    xs = x.reshape(x.shape[:-1] + (2, 2, half))
    bshape = (cos.shape[0],) + (1,) * extra + (2, half)
    c = cos.reshape(bshape).astype(x.dtype)
    s = sin.reshape(bshape).astype(x.dtype)
    x1, x2 = xs[..., 0, :], xs[..., 1, :]
    out = jnp.stack([x1 * c - x2 * s, x2 * c + x1 * s], axis=-2)
    return out.reshape(x.shape)

def pool_mixer(u, w, scale):
    B, L, D = u.shape
    t = jnp.arange(L)
    uf = u.astype(jnp.float32)
    csum = jnp.concatenate([jnp.zeros((B, 1, D), jnp.float32), lax.cumsum(uf, axis=1)], axis=1)
    outs = []
    for g, win in enumerate(POOL_WINDOWS):
        lo = jnp.clip(t - win // 2, 0, L)
        hi = jnp.clip(t + win // 2, 0, L)
        cs_g = csum[..., g * POOL_GW:(g + 1) * POOL_GW]
        cnt = (hi - lo).astype(jnp.float32)[None, :, None]
        outs.append((cs_g[:, hi] - cs_g[:, lo]) / cnt - uf[..., g * POOL_GW:(g + 1) * POOL_GW])
    pooled = jnp.stack(outs, axis=2).astype(u.dtype)
    y = jnp.einsum('blgc,gcd->blgd', pooled, w).reshape(B, L, D)
    return y * scale

def mla_queries(u, w_dq, q_norm, w_uq):
    B, L, _ = u.shape
    q = (rmsnorm(u @ w_dq, q_norm) @ w_uq).reshape(B, L, N_HEADS, QK_DIM)
    return q[..., :QK_NOPE], q[..., QK_NOPE:]

def mla_keys_values(u, w_dkv, kv_norm, w_ukv):
    B, L, _ = u.shape
    ckv = u @ w_dkv
    c_kv, k_rope = ckv[..., :KV_LORA], ckv[..., KV_LORA:]
    kv = (rmsnorm(c_kv, kv_norm) @ w_ukv).reshape(B, L, N_HEADS, QK_NOPE + V_DIM)
    return kv[..., :QK_NOPE], k_rope, kv[..., QK_NOPE:]

def attend(q_nope, q_rope, k_nope, k_rope, v):
    s = jnp.einsum('bqhd,bkhd->bhqk', q_nope, k_nope) + jnp.einsum('bqhr,bkr->bhqk', q_rope, k_rope)
    p = jax.nn.softmax(s.astype(jnp.float32) * ATTN_SCALE, axis=-1).astype(v.dtype)
    return jnp.einsum('bhqk,bkhd->bqhd', p, v)

def blocked_attention(q_nope, q_rope, k_nope, k_rope, v):
    B, L = q_nope.shape[:2]
    nb = L // Q_BLOCK

    def blocks(a):
        return jnp.moveaxis(a.reshape((B, nb, Q_BLOCK) + a.shape[2:]), 1, 0)

    out = lax.map(lambda qs: attend(qs[0], qs[1], k_nope, k_rope, v), (blocks(q_nope), blocks(q_rope)))
    return jnp.moveaxis(out, 0, 1).reshape(B, L, N_HEADS * V_DIM)

def mla_mixer(u, uc, cos, sin, w_dqkv, q_norm, w_uq, kv_norm, w_ukv, w_o, ctx_out):
    w_dq, w_dkv = w_dqkv[:, :Q_LORA], w_dqkv[:, Q_LORA:]
    qn, qr = mla_queries(u, w_dq, q_norm, w_uq)
    kn, kr, v = mla_keys_values(u, w_dkv, kv_norm, w_ukv)
    qr = apply_axial_rope(qr, cos, sin)
    kr = apply_axial_rope(kr, cos, sin)
    kn_c, kr_c, v_c = mla_keys_values(uc, w_dkv, kv_norm, w_ukv)
    k_nope = jnp.concatenate([kn_c, kn], axis=1)
    k_rope = jnp.concatenate([kr_c, kr], axis=1)
    vv = jnp.concatenate([v_c, v], axis=1)
    y = blocked_attention(qn, qr, k_nope, k_rope, vv) @ w_o
    yc = None
    if ctx_out:
        B, C = uc.shape[:2]
        qn_c, qr_c = mla_queries(uc, w_dq, q_norm, w_uq)
        yc = attend(qn_c, qr_c, kn_c, kr_c, v_c).reshape(B, C, N_HEADS * V_DIM) @ w_o
    return y, yc

def setup_inputs(seed: int = 0) -> dict:
    key = jax.random.key(seed)
    ks = jax.random.split(key, 18)
    D = D_MODEL

    def nrm(k, shape, scale):
        return jax.random.normal(k, shape, jnp.float32) * scale

    return {
        "x": nrm(ks[0], (BATCH, SEQ, D), 1.0),
        "c": nrm(ks[1], (BATCH, D), 1.0),
        "ctx": nrm(ks[2], (BATCH, CTX_LEN, D), 1.0),
        "c_ctx": nrm(ks[3], (D,), 1.0),
        "ada_w": nrm(ks[4], (DEPTH, D, N_MOD * D), 0.5 * D ** -0.5),
        "ada_b": nrm(ks[5], (DEPTH, N_MOD * D), 0.01),
        "norm_g": 1.0 + nrm(ks[6], (DEPTH, 4, D), 0.05),
        "pool_w": nrm(ks[7], (N_POOL_LAYERS, POOL_GROUPS, POOL_GW, POOL_GW), POOL_GW ** -0.5),
        "pool_scale": 1.0 + nrm(ks[8], (N_POOL_LAYERS, D), 0.1),
        "mla_w_dqkv": nrm(ks[9], (N_MLA_LAYERS, D, Q_LORA + KV_LORA + ROPE_DIM), D ** -0.5),
        "mla_q_norm": 1.0 + nrm(ks[10], (N_MLA_LAYERS, Q_LORA), 0.05),
        "mla_w_uq": nrm(ks[11], (N_MLA_LAYERS, Q_LORA, N_HEADS * QK_DIM), Q_LORA ** -0.5),
        "mla_kv_norm": 1.0 + nrm(ks[12], (N_MLA_LAYERS, KV_LORA), 0.05),
        "mla_w_ukv": nrm(ks[13], (N_MLA_LAYERS, KV_LORA, N_HEADS * (QK_NOPE + V_DIM)), KV_LORA ** -0.5),
        "mla_w_o": nrm(ks[14], (N_MLA_LAYERS, N_HEADS * V_DIM, D), (N_HEADS * V_DIM) ** -0.5),
        "ffn_w1": nrm(ks[15], (DEPTH, D, D_FF), D ** -0.5),
        "ffn_w3": nrm(ks[16], (DEPTH, D, D_FF), D ** -0.5),
        "ffn_w2": nrm(ks[17], (DEPTH, D_FF, D), D_FF ** -0.5),
    }

def reference(x, c, ctx, c_ctx, ada_w, ada_b, norm_g, pool_w, pool_scale, mla_w_dqkv, mla_q_norm,
              mla_w_uq, mla_kv_norm, mla_w_ukv, mla_w_o, ffn_w1, ffn_w3, ffn_w2):
    L = x.shape[1]
    cos, sin = axial_rope_tables(L)
    s_lat = jax.nn.silu(c)[:, None, :]
    s_ctx = jax.nn.silu(c_ctx)[None, None, :]
    h, hc = x, ctx
    for i in range(DEPTH):
        ctx_out = i < DEPTH - 1
        use_pool = i % N_MIXERS == 0
        j = i // N_MIXERS
        mod = jnp.split(s_lat @ ada_w[i] + ada_b[i], N_MOD, axis=-1)
        mod_c = jnp.split(s_ctx @ ada_w[i] + ada_b[i], N_MOD, axis=-1)
        u = modulate(rmsnorm(h, norm_g[i, 0]), mod[0], mod[1])
        if use_pool:
            y = pool_mixer(u, pool_w[j], pool_scale[j])
            if ctx_out:
                uc = modulate(rmsnorm(hc, norm_g[i, 0]), mod_c[0], mod_c[1])
                yc = pool_mixer(uc, pool_w[j], pool_scale[j])
        else:
            uc = modulate(rmsnorm(hc, norm_g[i, 0]), mod_c[0], mod_c[1])
            y, yc = mla_mixer(u, uc, cos, sin, mla_w_dqkv[j], mla_q_norm[j], mla_w_uq[j],
                              mla_kv_norm[j], mla_w_ukv[j], mla_w_o[j], ctx_out)
        h = h + mod[2] * rmsnorm(y, norm_g[i, 1])
        u = modulate(rmsnorm(h, norm_g[i, 2]), mod[3], mod[4])
        h = h + mod[5] * rmsnorm(swiglu(u, ffn_w1[i], ffn_w3[i], ffn_w2[i]), norm_g[i, 3])
        if ctx_out:
            hc = hc + mod_c[2] * rmsnorm(yc, norm_g[i, 1])
            uc = modulate(rmsnorm(hc, norm_g[i, 2]), mod_c[3], mod_c[4])
            hc = hc + mod_c[5] * rmsnorm(swiglu(uc, ffn_w1[i], ffn_w3[i], ffn_w2[i]), norm_g[i, 3])
    return h


_drawn_inputs = setup_inputs


def setup_inputs(seed=0):
    import zlib

    import numpy as np

    out = dict(_drawn_inputs(seed))
    spreads = {}
    factors = {'mla_q_norm': 8.0, 'mla_kv_norm': 3.955}
    for name, (base, spread) in spreads.items():
        noise = np.random.default_rng([zlib.crc32(name.encode()), seed]).standard_normal(out[name].shape)
        drawn = base * np.exp(spread * noise) if base else spread * noise
        out[name] = __import__('jax').numpy.asarray(drawn.astype(out[name].dtype))
    for name, factor in factors.items():
        out[name] = (out[name] * factor).astype(out[name].dtype)
    return out
```

```python
from contextlib import ExitStack

import numpy as np

import concourse.bass as bass
from concourse import mybir

F32 = mybir.dt.float32
F32R = mybir.dt.float32r
ALU = mybir.AluOpType
ACT = mybir.ActivationFunctionType
AX = mybir.AxisListType

P = 128
D = 2048
KT = D // P
SEQ, CTX = 256, 256
TOK = CTX + SEQ
DFF = 5632
EPS = 1e-6
N_MOD = 6
HEADS, NOPE, ROPE, VD = 16, 128, 64, 128
LORA = 512
LT = LORA // P
QK = NOPE + ROPE
SCALE = float(QK) ** -0.5
WINDOWS = (2, 4, 8, 16)
PAD = max(WINDOWS) // 2
GRID_W = 64
ROPE_BASE = 10000.0

RAW_SLOTS = 4
UNIT = 1024
CHUNK = 512
CHUNKS = N_MOD * D // CHUNK
ADA_U = KT * CHUNK // UNIT
FFN_IT = DFF // 256
W_U = KT * 256 // UNIT
W2_U = 2 * D // UNIT

N_TOK = 0
N_ADA0 = N_TOK + 8
N_POOL, M_POOL = N_ADA0 + CHUNKS * ADA_U, 0
N_FFN0, M_FFN0 = N_POOL + 8, M_POOL + 8
ADA_LOOPED = FFN_IT
N_ADA1 = N_FFN0 + FFN_IT * (2 * W_U + W2_U + ADA_U)
N_DQKV, M_DQKV = N_ADA1 + (CHUNKS - ADA_LOOPED) * ADA_U, M_FFN0 + FFN_IT * (2 * W_U + W2_U)
DQKV_U = 4 * 4 + 2
N_HEADS, M_HEADS = N_DQKV + DQKV_U, M_DQKV + DQKV_U
N_WO, M_WO = N_HEADS + 2 * HEADS, M_HEADS + 2 * HEADS
N_FFN1, M_FFN1 = N_WO + 32, M_WO + 32


def program(nc, x, ctx, c, c_ctx, ada_w, ada_b, norm_g, pool_w, pool_scale, w_dqkv, q_norm, w_uq,
            kv_norm, w_ukv, w_o, ffn_w1, ffn_w3, ffn_w2, mats, rope_tables, pool_inv, out):
    stack = ExitStack()

    def sem(name):
        return stack.enter_context(nc.semaphore(name))

    base = (nc.sbuf_base + 63) // 64 * 64

    def at(name, offset, shape, dt=F32):
        return nc.alloc_sbuf_tensor_at(name, [P] + shape, dt, offset=base + offset)

    KB = 1024
    Y_AT, H_AT, U_AT, HC_AT, RAW_AT, SPLIT_AT, MISC_AT = (k * KB for k in (0, 32, 64, 128, 144, 160, 192))
    Y = at("mixer_or_ffn_out", Y_AT, [KT, TOK])
    H = at("stream", H_AT, [KT, TOK])
    U = at("sublayer_in_hilo", U_AT, [2, KT, TOK], F32R)
    HC = at("ffn_hidden_hilo", HC_AT, [2, 2, 2, TOK], F32R)
    RAW = at("raw_units", RAW_AT, [RAW_SLOTS, UNIT])
    SPL = at("split_units", SPLIT_AT, [RAW_SLOTS, 2, UNIT], F32R)
    off = [MISC_AT]

    def misc(name, shape):
        t = at(name, off[0], shape)
        off[0] += (4 * int(np.prod(shape)) + 31) // 32 * 32
        return t

    MATS = misc("const_mats", [P + 2 + P])
    MOD = misc("mod_cols", [2, 2, N_MOD * KT])
    COL = misc("scale_gate_cols", [8, 2, KT])
    VEC = misc("param_cols", [P + 2 * 96 + 56])
    SIL = misc("silu_cols", [KT, 32])
    RSTD = misc("rstd", [TOK])
    ACC = misc("square_sum", [TOK])
    SQ = misc("squares", [2, TOK])
    SMALL = misc("softmax_cols", [4, 4])
    ONES = misc("ones", [P])
    assert base + off[0] <= nc.sbuf_usable_end, (off[0], nc.sbuf_usable_end)
    IDENT, SEL, SWAP = MATS[:, 0:P], MATS[:, P:P + 2], MATS[:, P + 2:P + 2 + P]
    G_COL, B_COL, S_COL = 0, P, P + 192
    PS_COL, QN_COL, KVN_COL = S_COL + 32, S_COL + 48, S_COL + 52
    PINV = at("pool_inverse_counts", Y_AT + 28 * KB, [4, SEQ])
    ROWS = at("param_rows", HC_AT, [4, P])
    TMP = at("norm_tmp", HC_AT, [2, TOK])
    PU = at("pool_padded", HC_AT + 4 * KB, [2, SEQ + 2 * PAD])
    PA = at("pool_sum_a", HC_AT + 4 * KB + 2176, [2, SEQ + 2 * PAD])
    PB = at("pool_sum_b", HC_AT + 4 * KB + 2 * 2176, [2, SEQ + 2 * PAD])
    PD = at("pool_difference", HC_AT + 4 * KB + 3 * 2176, [TOK])
    CQ = at("q_latent", Y_AT, [LT, SEQ])
    CKV = at("kv_latent", Y_AT + 4 * KB, [LT, TOK])
    KRAW = at("k_rope_raw", Y_AT + 12 * KB, [TOK])
    LSQ_Q = at("q_latent_squares", Y_AT + 14 * KB, [LT, SEQ])
    LSQ_KV = at("kv_latent_squares", Y_AT + 18 * KB, [LT, TOK])
    KROT = at("k_rope_rotated", Y_AT + 26 * KB, [SEQ])
    KSIN = at("k_rope_sin_part", Y_AT + 27 * KB, [SEQ])
    RSTDQ = at("rstd_q", Y_AT + 28 * KB, [SEQ])
    OT = at("attn_out_hilo", Y_AT, [2, HEADS, SEQ], F32R)
    KVL = at("kv_latent_hilo", U_AT, [2, LT, TOK], F32R)
    QL = at("q_latent_hilo", U_AT + 16 * KB, [2, LT, SEQ], F32R)
    QN = at("q_nope_hilo", U_AT + 24 * KB, [2, 2, SEQ], F32R)
    QR = at("q_rope_hilo", U_AT + 28 * KB, [2, 2, SEQ], F32R)
    KN = at("k_nope_hilo", U_AT + 32 * KB, [2, 2, TOK], F32R)
    V = at("v_hilo", U_AT + 40 * KB, [2, 2, 2, TOK], F32R)
    PT = at("probs_T_hilo", U_AT + 56 * KB, [2, 4, SEQ], F32R)
    KR = at("k_rope_hilo", HC_AT, [2, TOK], F32R)
    PR = at("probs", HC_AT + 4 * KB, [2, 2, TOK])
    QF = at("q_rope_raw", HC_AT + 12 * KB, [SEQ])
    QS = at("q_rope_sin_part", HC_AT + 13 * KB, [SEQ])
    Y1 = at("attn_projected", U_AT + 48 * KB, [KT, SEQ])
    COS, SIN = H[:, 0, 0:SEQ], H[:, 1, 0:SEQ]
    OUTT = at("out_rows", U_AT, [2, D])

    PS = [stack.enter_context(nc.psum_tensor(f"bank{b}", [P, 512], F32)) for b in range(8)]

    raw_full = [sem(f"raw_full{s}") for s in range(RAW_SLOTS)]
    raw_done = [sem(f"raw_done{s}") for s in range(RAW_SLOTS)]
    hi_ready = sem("hi_ready")
    mult_done = sem("mult_done")
    consts_in, rows_in, tables_in, pinv_in = sem("consts_in"), sem("rows_in"), sem("tables_in"), sem("pinv_in")
    ones_ready, sil_zero = sem("ones_ready"), sem("sil_zero")
    vec_T, vec_ready, sil_ready = sem("vec_T"), sem("vec_ready"), sem("sil_ready")
    tok_T, tok_a, tok_b = sem("tok_T"), sem("tok_a"), sem("tok_b")
    ada_row, sel_done, mod_ready = sem("ada_row"), sem("sel_done"), sem("mod_ready")
    col_ready = sem("col_ready")
    out_stored = sem("out_stored")

    def stage_sems(name, *parts):
        return {s: sem(f"{name}_{s}") for s in parts}

    stats = stage_sems("stats", "sq", "acc", "ss", "var", "std", "rstd")

    def norm_stage(k, *parts):
        s = {p: sem(f"norm{k}_{p}") for p in parts}
        s.update(stats)
        s.update(sq0=k * KT, acc0=k * (KT + 2), one0=k)
        return s

    n0 = norm_stage(0)
    norm01, norm02 = norm_stage(1, "t", "h"), norm_stage(2, "t", "hi", "lo")
    norm03, norm10 = norm_stage(3, "t", "h"), norm_stage(4, "t", "hi", "lo")
    norm11, norm12 = norm_stage(5, "t", "h"), norm_stage(6, "t", "hi", "lo")
    norm13 = norm_stage(7, "t", "h")
    pool = {k: sem(f"pool_{k}") for k in ("t", "u", "partial", "s", "m", "d", "hi", "lo", "y")}
    ffn = [{k: sem(f"ffn{l}_{k}") for k in ("silu", "hf", "hi", "lo", "y", "y_free")} for l in range(2)]
    dq = {k: sem(f"dqkv_{k}") for k in ("evac", "sq", "ss", "var", "std", "rstd", "t", "hi", "lo",
                                        "swap", "sin", "cos", "rot", "krhi", "krlo")}
    hd = {k: sem(f"head_{k}") for k in ("qpe", "qn_hi", "qn_lo", "qf", "swap", "sin", "cos", "rot", "qr_hi",
                                        "qr_lo", "kpe", "kn_hi", "kn_lo", "v_hi", "v_lo", "s", "max",
                                        "nmax", "exp", "rinv", "p", "pt", "pt_hi", "pt_lo", "o",
                                        "o_hi", "o_lo", "qr_zero")}
    wo_y = sem("wo_y")
    out_T, out_a, out_b = sem("out_T"), sem("out_a"), sem("out_b")

    block = stack.enter_context(nc.Block())

    both = [(0, 0, CTX), (1, CTX, SEQ)]
    latent = [(1, CTX, SEQ)]

    def ffn_units(l):
        return 2 * W_U + W2_U + (ADA_U if l == 0 else 0)

    def unit_parts(n, m):
        raw = RAW[:, n % RAW_SLOTS, :]
        slot = m % RAW_SLOTS
        if M_DQKV + 16 <= m < M_DQKV + DQKV_U:
            return [(raw[:, 0:8 * ROPE].rearrange("p (k r) -> p k r", k=8).unsqueeze(2).to_broadcast([P, 8, 2, ROPE]),
                     lambda hl: SPL[:, slot, hl, :].rearrange("p (k h r) -> p k h r", k=8, h=2))]
        if M_HEADS <= m < M_WO and (m - M_HEADS) % 4 < 2:
            cols = raw[:, 0:4 * QK].rearrange("p (k h q) -> p k h q", k=2, h=2)

            def split(hl, lo, hi):
                return SPL[:, slot, hl, 0:4 * QK].rearrange("p (k q) -> p k q", k=2)[:, :, lo:hi].rearrange(
                    "p k (h q) -> p k h q", h=2)

            return [(cols[:, :, :, 0:NOPE], lambda hl: split(hl, 0, 2 * NOPE)),
                    (cols[:, :, :, NOPE:QK], lambda hl: split(hl, 2 * NOPE, 2 * QK))]
        return [(raw, lambda hl: SPL[:, slot, hl, :])]

    def ffn_place(l, t):
        return t + (min(t, ADA_U) if l == 0 else 0)

    def ffn_ahead(l, t, up_only, last=False):
        size = 2 * W_U + (0 if up_only else W2_U)
        if t + 4 >= size:
            ahead = t + 4 - size
            return ffn_units(l) - (W2_U if up_only else 0) + (ahead if last else ffn_place(l, ahead))
        return ffn_place(l, t + 4)

    def full_wait(eng, n, rt=0):
        eng.wait_ge(raw_full[n % RAW_SLOTS], 16 * (n // RAW_SLOTS + 1) + 16 * rt)

    @block.sync
    def _(sp):
        sp.dma_start(MATS[:, :], mats).then_inc(consts_in, 16)

        def load(n, src, dst=None, rt=0):
            slot = n % RAW_SLOTS
            if n >= RAW_SLOTS:
                sp.wait_ge(raw_done[slot], n // RAW_SLOTS + rt)
            sp.dma_start(RAW[:, slot, :] if dst is None else dst, src).then_inc(raw_full[slot], 16)

        def tiled(n, k, w):
            return RAW[:, n % RAW_SLOTS, 0:k * w].rearrange("p (k w) -> p k w", k=k)

        def load_chunk(n, l, chunk, rt=0):
            for q in range(ADA_U):
                load_chunk_unit(n + q, l, chunk, q, rt)

        def load_chunk_unit(n, l, chunk, q, rt=0):
            w = ada_w[l].rearrange("(k p) n -> p k n", p=P)
            load(n, w[:, 2 * q:2 * q + 2, bass.ds(chunk * CHUNK, CHUNK)], tiled(n, 2, CHUNK), rt)

        for n in range(8):
            src = (ctx if n < 4 else x)[0].rearrange("(t p) d -> t p d", p=P)[(n // 2) % 2]
            load(N_TOK + n, src[:, (n % 2) * UNIT:(n % 2 + 1) * UNIT])
            if n == 1:
                sp.dma_start(ROWS[:, 0, :], norm_g.rearrange("a b (k p) -> (a b k) p", p=P)).then_inc(rows_in, 16)
                for l in range(2):
                    sp.dma_start(ROWS[0:96, 1 + l, :], ada_b[l].rearrange("(k p) -> k p", p=P)).then_inc(rows_in, 16)
                r = 0
                for v in (c[0], c_ctx, pool_scale[0], q_norm[0], kv_norm[0]):
                    k = v.shape[0] // P
                    sp.dma_start(ROWS[r:r + k, 3, :], v.rearrange("(k p) -> k p", p=P)).then_inc(rows_in, 16)
                    r += k
        sp.dma_start(PINV[:, :, :], pool_inv.rearrange("p (g t) -> p g t", g=4)).then_inc(pinv_in, 16)
        with sp.Fori(0, CHUNKS // 2) as i:
            for b in range(2):
                load_chunk(N_ADA0 + b * ADA_U, 0, 2 * i + b, i * (2 * ADA_U // RAW_SLOTS))
        for u in range(8):
            load(N_POOL + u, pool_w[0, u // 2].rearrange("(k p) n -> p k n", p=P)[:, 2 * (u % 2):2 * (u % 2) + 2, :],
                 tiled(N_POOL + u, 2, 512))

        def load_ffn(l, n_base):
            w13 = [w[l].rearrange("(k p) n -> p k n", p=P) for w in (ffn_w1, ffn_w3)]
            w2 = ffn_w2[l].rearrange("(f p) n -> p f n", p=P)

            def up(n, i, rt=0):
                for t in range(2 * W_U):
                    u, k = t % W_U, n + ffn_place(l, t)
                    load(k, w13[t // W_U][:, 4 * u:4 * u + 4, bass.ds(i * 256, 256)], tiled(k, 4, 256), rt)
                    if l == 0:
                        load_chunk_unit(k + 1, 1, i, t, rt)
                return n + ffn_place(l, 2 * W_U)

            def down(n, i, rt=0):
                for u in range(W2_U):
                    load(n + u, w2[:, bass.ds(i * 2, 2), 512 * u:512 * u + 512], tiled(n + u, 2, 512), rt)

            step = ffn_units(l)
            n = up(n_base, 0)
            with sp.Fori(0, (FFN_IT - 2) // 2) as j:
                for b in range(2):
                    rt = j * (2 * step // RAW_SLOTS)
                    down(up(n + b * step, 2 * j + 1 + b, rt), 2 * j + b, rt)
            n += (FFN_IT - 2) * step
            down(up(n, FFN_IT - 1), FFN_IT - 2)
            down(n + step, FFN_IT - 1)

        load_ffn(0, N_FFN0)
        for k in range(CHUNKS - ADA_LOOPED):
            load_chunk(N_ADA1 + k * ADA_U, 1, ADA_LOOPED + k)
        dqkv = w_dqkv[0].rearrange("(k p) n -> p k n", p=P)
        for u in range(16):
            n = N_DQKV + u
            load(n, dqkv[:, 4 * (u % 4):4 * (u % 4) + 4, 256 * (u // 4):256 * (u // 4) + 256], tiled(n, 4, 256))
        for u in range(2):
            load(N_DQKV + 16 + u, dqkv[:, 8 * u:8 * u + 8, 2 * LORA:2 * LORA + ROPE], tiled(N_DQKV + 16 + u, 8, ROPE))
        sp.wait_ge(norm10["hi"], KT)
        sp.wait_ge(norm10["lo"], KT)
        sp.dma_start(COS, rope_tables[:, 0:SEQ]).then_inc(tables_in, 16)
        sp.dma_start(SIN, rope_tables[:, SEQ:2 * SEQ]).then_inc(tables_in, 16)
        uq = w_uq[0].rearrange("(k p) n -> p k n", p=P)
        ukv = w_ukv[0].rearrange("(k p) n -> p k n", p=P)
        with sp.Fori(0, HEADS // 2) as pair:
            for u in range(2):
                n = N_HEADS + u
                load(n, uq[:, 2 * u:2 * u + 2, bass.ds(pair * (2 * QK), 2 * QK)], tiled(n, 2, 2 * QK), pair)
            for a in range(2):
                n = N_HEADS + 2 + a
                load(n, ukv[:, :, bass.ds(pair * 512 + a * 256, 256)], tiled(n, LT, 256), pair)
        wo = w_o[0].rearrange("(k p) n -> p k n", p=P)
        with sp.Fori(0, 4) as j:
            for b in range(2):
                for u in range(4):
                    n = N_WO + 4 * b + u
                    load(n, wo[:, 4 * u:4 * u + 4, bass.ds(j * 512 + b * 256, 256)], tiled(n, 4, 256), j * 2)
        load_ffn(1, N_FFN1)
        for t in range(2):
            sp.wait_ge(out_a, 2 * (t + 1))
            sp.wait_ge(out_b, 2 * (t + 1))
            sp.dma_start(out[0, t * P:(t + 1) * P, :], OUTT[:, t, :]).then_inc(out_stored, 16)
        sp.wait_ge(out_stored, 32)

    @block.tensor
    def _(pe):
        def mac3(ps, w_hi, w_lo, x_hi, x_lo, first, last):
            nc.tensor.matmul(ps, w_hi, x_hi, start=first, stop=False)
            nc.tensor.matmul(ps, w_hi, x_lo, start=False, stop=False)
            return nc.tensor.matmul(ps, w_lo, x_hi, start=False, stop=last)

        def split_wait(n, rt=0):
            pe.wait_ge(raw_done[n % RAW_SLOTS], n // RAW_SLOTS + 1 + rt)

        def unit(m):
            return SPL[:, m % RAW_SLOTS, 0, :], SPL[:, m % RAW_SLOTS, 1, :]

        def ada_product(n, bank, rt=0):
            for q in range(ADA_U):
                ada_unit(n + q, q, bank, rt)

        def ada_unit(n, q, bank, rt=0):
            full_wait(pe, n, rt)
            for k2 in range(2):
                kt = 2 * q + k2
                g = kt % 4
                mm = nc.tensor.matmul(bank[32 * g:32 * g + 32, :], SIL[:, kt, :],
                                      RAW[:, n % RAW_SLOTS, k2 * CHUNK:(k2 + 1) * CHUNK],
                                      start=kt < 4, stop=kt >= KT - 4, tile_position=(0, 32 * g))
            mm.then_inc(raw_done[n % RAW_SLOTS], 1)

        def ada_select(row, bank):
            for t in range(4):
                mm = nc.tensor.matmul(bank[:, 2 * t:2 * t + 2], row[:, P * t:P * t + P], SEL, start=True, stop=True)
            mm.then_inc(sel_done, 1)

        def square_sum(s, n_tok):
            pe.wait_ge(s["acc"], s["acc0"] + KT + 2)
            nc.tensor.matmul(PS[7][:, 0:n_tok], ONES[:, :], ACC[:, 0:n_tok], start=True, stop=True).then_inc(s["ss"], 1)

        pe.wait_ge(consts_in, 16)
        pe.wait_ge(rows_in, 16 * 8)
        nc.tensor.transpose(PS[4][:, 0:P], ROWS[:, 0, :], IDENT)
        nc.tensor.transpose(PS[4][:, P:P + 96], ROWS[0:96, 1, :], IDENT[0:96, 0:96])
        nc.tensor.transpose(PS[4][:, P + 96:P + 192], ROWS[0:96, 2, :], IDENT[0:96, 0:96])
        nc.tensor.transpose(PS[4][:, S_COL:S_COL + 56], ROWS[0:56, 3, :], IDENT[0:56, 0:56]).then_inc(vec_T, 1)
        for n in range(8):
            full_wait(pe, n)
            if n >= 2:
                pe.wait_ge(tok_a, n - 1)
                pe.wait_ge(tok_b, n - 1)
            for half in range(2):
                for t in range(4):
                    f = (4 * half + t) * P
                    mm = nc.tensor.transpose(PS[2 * (n % 2) + half][:, t * P:(t + 1) * P],
                                             RAW[:, n % RAW_SLOTS, f:f + P], IDENT)
                mm.then_inc(tok_T if half == 0 else raw_done[n % RAW_SLOTS], 1)
        pe.wait_ge(ones_ready, 1)
        square_sum(n0, TOK)

        pe.wait_ge(sil_ready, 2)
        pe.wait_ge(tok_a, 8)
        pe.wait_ge(tok_b, 8)

        def chunk0(n, b, chunk, rt=0, waits=True):
            if waits:
                pe.wait_ge(ada_row, chunk - 1)
            ada_product(n, PS[b], rt)

        def select0(b, chunk, waits=True):
            pe.wait_ge(ada_row, chunk + 1)
            if waits:
                pe.wait_ge(mod_ready, 2 * (chunk - 1))
            ada_select(SQ[:, b, :], PS[2 + b])

        chunk0(N_ADA0, 0, 0, waits=False)
        chunk0(N_ADA0 + ADA_U, 1, 1, waits=False)
        select0(0, 0, waits=False)
        chunk0(N_ADA0 + 2 * ADA_U, 0, 2)
        select0(1, 1, waits=False)
        with pe.Fori(0, CHUNKS // 2 - 2) as j:
            for b in range(2):
                chunk0(N_ADA0 + (3 + b) * ADA_U, (1 + b) % 2, 2 * j + 3 + b, j * (2 * ADA_U // RAW_SLOTS))
                select0(b, 2 * j + 2 + b)
        chunk0(N_ADA0 + (CHUNKS - 1) * ADA_U, 1, CHUNKS - 1)
        select0(0, CHUNKS - 2)
        select0(1, CHUNKS - 1)

        for u in range(8):
            g, m = u // 2, M_POOL + u
            split_wait(N_POOL + u)
            pe.wait_ge(pool["lo"], 2 * (u + 1))
            w_hi, w_lo = unit(m)
            if u % 2 == 0:
                if g < 2:
                    pe.wait_ge(mod_ready, 2 * CHUNKS)
                else:
                    pe.wait_ge(pool["y"], 4 * (g - 1))
            for k2 in range(2):
                kt = 2 * u + k2
                for t in range(4):
                    f = k2 * 512 + t * P
                    mm = mac3(PS[4 * (g % 2) + t][:, :], w_hi[:, f:f + P], w_lo[:, f:f + P],
                              U[:, 0, kt, :], U[:, 1, kt, :], kt % 4 == 0, kt % 4 == 3)
            mm.then_inc(mult_done, 1)

        def run_ffn(l, n_base, m_base, norm, c0, nt):
            s = ffn[l]
            step = ffn_units(l)

            def up(n, m, i, rt=0, first=False):
                if not first:
                    pe.wait_ge(s["silu"], 2 * i)
                    if l == 0:
                        pe.wait_ge(s["y_free"], 4 + 16 * (i - 1))
                for t in range(2 * W_U):
                    mat, u = t // W_U, t % W_U
                    k = n + ffn_place(l, t)
                    if t == W_U and not first:
                        pe.wait_ge(s["hf"], 2 * i)
                    split_wait(k, rt)
                    if first and mat == 0:
                        pe.wait_ge(norm["lo"], 4 * u + 4)
                    w_hi, w_lo = unit(m + t)
                    for k4 in range(4):
                        kt = 4 * u + k4
                        for a in range(2):
                            f = k4 * 256 + a * P
                            mm = mac3(PS[2 * mat + a][:, 0:nt], w_hi[:, f:f + P], w_lo[:, f:f + P],
                                      U[:, 0, kt, c0:c0 + nt], U[:, 1, kt, c0:c0 + nt], kt == 0, kt == KT - 1)
                    mm.then_inc(mult_done, 1)
                    if l == 0:
                        ada_unit(k + 1, t, PS[4], rt)
                if l == 0:
                    pe.wait_ge(ada_row, CHUNKS + i + 1)
                    ada_select(ACC[:, :], PS[5])
                return n + ffn_place(l, 2 * W_U), m + 2 * W_U

            def down(n, m, i, slot, rt=0, ada=True):
                pe.wait_ge(s["lo"], 2 * (i + 1))
                if l == 0 and ada:
                    pe.wait_ge(mod_ready, 2 * (CHUNKS + i + 2))
                for u in range(W2_U):
                    split_wait(n + u, rt)
                    w_hi, w_lo = unit(m + u)
                    for b in range(4):
                        pe.wait_ge(s["y_free"], 16 * i + 4 * u + b + 1)
                        for f2 in range(2):
                            f = f2 * 512 + b * P
                            mm = mac3(PS[4 + b][:, 0:nt], w_hi[:, f:f + P], w_lo[:, f:f + P],
                                      HC[:, slot, 0, f2, 0:nt], HC[:, slot, 1, f2, 0:nt], f2 == 0, f2 == 1)
                        mm.then_inc(s["y"] if b < 3 else mult_done, 1)

            n, m = up(n_base, m_base, 0, first=True)
            with pe.Fori(0, (FFN_IT - 2) // 2) as j:
                for b in range(2):
                    rt = j * (2 * step // RAW_SLOTS)
                    nn, mm_ = up(n + b * step, m + 12 * b, 2 * j + 1 + b, rt)
                    down(nn, mm_, 2 * j + b, b, rt)
            n, m = n + (FFN_IT - 2) * step, m + (FFN_IT - 2) * 12
            nn, mm_ = up(n, m, FFN_IT - 1)
            down(nn, mm_, FFN_IT - 2, 0)
            down(n + step, m + 12, FFN_IT - 1, 1, ada=False)

        square_sum(norm01, TOK)
        square_sum(norm02, TOK)
        run_ffn(0, N_FFN0, M_FFN0, norm02, 0, TOK)

        for k in range(CHUNKS - ADA_LOOPED):
            chunk = CHUNKS + ADA_LOOPED + k
            pe.wait_ge(ffn[0]["y_free"], 4 + 16 * FFN_IT)
            pe.wait_ge(mod_ready, 2 * chunk)
            ada_product(N_ADA1 + k * ADA_U, PS[4])
            pe.wait_ge(ada_row, chunk + 1)
            ada_select(ACC[:, :], PS[5])
        square_sum(norm03, TOK)
        square_sum(norm10, TOK)

        for pr in range(4):
            c0, nt = (CTX, SEQ) if pr < 2 else (0, TOK)
            for u in range(4):
                m = M_DQKV + 4 * pr + u
                split_wait(N_DQKV + 4 * pr + u)
                if pr == 0:
                    pe.wait_ge(norm10["lo"], 4 * u + 4)
                w_hi, w_lo = unit(m)
                for k4 in range(4):
                    kt = 4 * u + k4
                    for a in range(2):
                        f = k4 * 256 + a * P
                        mm = mac3(PS[2 * pr + a][:, 0:nt], w_hi[:, f:f + P], w_lo[:, f:f + P],
                                  U[:, 0, kt, c0:c0 + nt], U[:, 1, kt, c0:c0 + nt], kt == 0, kt == KT - 1)
                mm.then_inc(mult_done, 1)
        pe.wait_ge(dq["evac"], 2)
        for u in range(2):
            split_wait(N_DQKV + 16 + u)
            w_hi, w_lo = unit(M_DQKV + 16 + u)
            for k8 in range(8):
                kt = 8 * u + k8
                mm = mac3(PS[0][:, :], w_hi[:, k8 * P:k8 * P + P], w_lo[:, k8 * P:k8 * P + P],
                          U[:, 0, kt, :], U[:, 1, kt, :], kt == 0, kt == KT - 1)
            mm.then_inc(mult_done, 1)
        pe.wait_ge(dq["sq"], 2)
        for kt in range(LT):
            nc.tensor.matmul(PS[2][:, 0:SEQ], ONES[:, :], LSQ_Q[:, kt, :], start=kt == 0, stop=kt == LT - 1)
        for kt in range(LT):
            mm = nc.tensor.matmul(PS[3][:, :], ONES[:, :], LSQ_KV[:, kt, :], start=kt == 0, stop=kt == LT - 1)
        mm.then_inc(dq["ss"], 1)
        pe.wait_ge(dq["evac"], 9)
        nc.tensor.matmul(PS[4][:, 0:SEQ], SWAP, KRAW[:, CTX:TOK], start=True, stop=True).then_inc(dq["swap"], 1)

        def project(pair, m, rt=0, first=False, vslot=0):
            n = N_HEADS + (m - M_HEADS)
            split_wait(n, rt)
            split_wait(n + 1, rt)
            if first:
                pe.wait_ge(dq["lo"], 8)
                pe.wait_ge(dq["krlo"], 1)
                pe.wait_ge(dq["krhi"], 1)
            else:
                pe.wait_ge(hd["qn_lo"], pair)
                pe.wait_ge(hd["sin"], pair)
                pe.wait_ge(hd["o_lo"], 2 * pair - 2 if not isinstance(pair, int) else max(0, 2 * pair - 2))
            units = [unit(m), unit(m + 1)]

            def cols(k, hl, part):
                w = units[k // 2][hl]
                return w[:, (k % 2) * 2 * QK + part * P:(k % 2) * 2 * QK + (part + 1) * P]

            for part in range(3):
                ps = PS[0][:, part * SEQ:(part + 1) * SEQ] if part < 2 else PS[1][:, 0:SEQ]
                for k in range(LT):
                    mm = mac3(ps, cols(k, 0, part), cols(k, 1, part), QL[:, 0, k, :], QL[:, 1, k, :], k == 0, k == LT - 1)
            mm.then_inc(mult_done, 2)
            for a in range(2):
                split_wait(n + 2 + a, rt)
                w_hi, w_lo = unit(m + 2 + a)
                if not (first and a == 0):
                    pe.wait_ge(hd["kn_lo"], 2 * pair + a)
                for k in range(LT):
                    mm = mac3(PS[2][:, :], w_hi[:, k * 256:k * 256 + P], w_lo[:, k * 256:k * 256 + P],
                              KVL[:, 0, k, :], KVL[:, 1, k, :], k == 0, k == LT - 1)
                mm.then_inc(hd["kpe"], 1)
                if not (first and a == 0):
                    pe.wait_ge(hd["v_lo"], 2 * pair + a)
                for j in range(4):
                    for k in range(LT):
                        f = k * 256 + P
                        mm = mac3(PS[3][:, j * P:(j + 1) * P], KVL[:, 0, k, j * P:(j + 1) * P],
                                  KVL[:, 1, k, j * P:(j + 1) * P], w_hi[:, f:f + P], w_lo[:, f:f + P],
                                  k == 0, k == LT - 1)
                mm.then_inc(mult_done, 1)
                if a == 0:
                    pe.wait_ge(hd["qf"], pair + 1)
                    nc.tensor.matmul(PS[1][:, SEQ:2 * SEQ], SWAP, QF[:, :], start=True, stop=True).then_inc(hd["swap"], 1)

        def scores(pair, a, first=False):
            h = 2 * pair + a
            if first:
                pe.wait_ge(hd["qr_zero"], 2)
            if a == 0:
                pe.wait_ge(hd["qn_lo"], pair + 1)
                pe.wait_ge(hd["qr_lo"], pair + 1)
            pe.wait_ge(hd["kn_lo"], h + 1)
            for qt in range(2):
                if not (first and a == 0):
                    pe.wait_ge(hd["exp"], 2 * h - 1 + qt)
                q = slice(qt * P, (qt + 1) * P)
                mac3(PS[4 + qt][:, :], QN[:, 0, a, q], QN[:, 1, a, q], KN[:, 0, a, :], KN[:, 1, a, :], True, False)
                mac3(PS[4 + qt][:, :], QR[:, 0, a, q], QR[:, 1, a, q], KR[:, 0, :], KR[:, 1, :],
                     False, True).then_inc(hd["s"], 1)

        def weigh(pair, a, vslot, first=False):
            h = 2 * pair + a
            for qt in range(2):
                pe.wait_ge(hd["p"], 2 * h + qt + 1)
                if not (first and a == 0):
                    pe.wait_ge(hd["pt_lo"], 2 * h - 1 + qt)
                for j in range(4):
                    mm = nc.tensor.transpose(PS[6 + qt][:, j * P:(j + 1) * P], PR[:, a, qt, j * P:(j + 1) * P], IDENT)
                mm.then_inc(hd["pt"], 1)
            pe.wait_ge(hd["pt_lo"], 2 * h + 2)
            pe.wait_ge(hd["v_lo"], h + 1)
            pe.wait_ge(hd["sin"], pair + 1)
            if not (first and a == 0):
                pe.wait_ge(hd["o_lo"], h)
            for j in range(4):
                mm = mac3(PS[1][:, a * SEQ:(a + 1) * SEQ], V[:, vslot, 0, a, j * P:(j + 1) * P],
                          V[:, vslot, 1, a, j * P:(j + 1) * P], PT[:, 0, j, :], PT[:, 1, j, :], j == 0, j == 3)
            mm.then_inc(hd["o"], 1)

        def head_pair(pair, m, vslot, rt=0, first_weigh=False):
            project(pair, m, rt)
            for a in range(2):
                if a == 0:
                    pe.wait_ge(hd["sin"], pair + 1)
                weigh(pair - 1, a, 1 - vslot, first=first_weigh)
                scores(pair, a)

        project(0, M_HEADS, first=True)
        scores(0, 0, first=True)
        scores(0, 1, first=True)
        head_pair(1, M_HEADS + 4, 1, first_weigh=True)
        with pe.Fori(0, 3) as j:
            for b in range(2):
                head_pair(2 * j + 2 + b, M_HEADS + 8 + 4 * b, b, j * 2)
        weigh(HEADS // 2 - 1, 0, 1)
        weigh(HEADS // 2 - 1, 1, 1)

        pe.wait_ge(hd["o_lo"], HEADS)

        def project_out(n, m, dp, bank, rt=0, waits=True):
            for u in range(4):
                split_wait(n + u, rt)
                if u == 0 and waits:
                    pe.wait_ge(wo_y, 2 * dp - 2)
                w_hi, w_lo = unit(m + u)
                for k4 in range(4):
                    h = 4 * u + k4
                    for a in range(2):
                        f = k4 * 256 + a * P
                        mm = mac3(PS[bank + a][:, 0:SEQ], w_hi[:, f:f + P], w_lo[:, f:f + P],
                                  OT[:, 0, h, :], OT[:, 1, h, :], h == 0, h == HEADS - 1)
                mm.then_inc(mult_done, 1)

        project_out(N_WO, M_WO, 0, 2, waits=False)
        project_out(N_WO + 4, M_WO + 4, 1, 4)
        with pe.Fori(0, 3) as j:
            for b in range(2):
                project_out(N_WO + 8 + 4 * b, M_WO + 8 + 4 * b, 2 * j + 2 + b, 2 + 2 * b, j * 2)

        square_sum(norm11, SEQ)
        square_sum(norm12, SEQ)
        run_ffn(1, N_FFN1, M_FFN1, norm12, CTX, SEQ)
        square_sum(norm13, SEQ)
        for t in range(2):
            for q in range(4):
                pe.wait_ge(norm13["h"], 4 * q + 4)
                if t == 0 and q == 0:
                    pe.wait_ge(norm13["rstd"], norm13["one0"] + 1)
                for j in range(4):
                    kt = 4 * q + j
                    mm = nc.tensor.transpose(PS[4 * t + q][:, j * P:(j + 1) * P],
                                             H[:, kt, CTX + t * P:CTX + (t + 1) * P], IDENT)
                mm.then_inc(out_T, 1)

    @block.scalar
    def _(act):
        def split_hi(n, m, rt=0, mt=0):
            full_wait(act, n, rt)
            if m >= RAW_SLOTS:
                act.wait_ge(mult_done, m - RAW_SLOTS + 1 + mt * RAW_SLOTS)
            for raw, split in unit_parts(n, m):
                ins = nc.scalar.activation(split(0), raw, ACT.Copy)
            ins.then_inc(hi_ready, 1)

        def copy(dst, src):
            return nc.scalar.activation(dst, src, ACT.Copy)

        def squares(s, src, src_ready, n_tok):
            with act.Fori(0, KT // 2) as j:
                for b in range(2):
                    kt = 2 * j + b
                    if src_ready is not None:
                        act.wait_ge(src_ready, kt + 1)
                    act.wait_ge(s["acc"], s["acc0"] + kt + 1)
                    nc.scalar.activation(SQ[:, b, 0:n_tok], src(kt), ACT.Square).then_inc(s["sq"], 1)

        def root(s, n_tok):
            act.wait_ge(s["var"], s["one0"] + 1)
            nc.scalar.activation(RSTD[:, 0:n_tok], ACC[:, 0:n_tok], ACT.Sqrt).then_inc(s["std"], 1)

        def apply_hi(s, l, shift, segs):
            def tile(kt, b):
                act.wait_ge(s["t"], kt + 1)
                for q, c0, w in segs:
                    ins = nc.scalar.activation(U[:, 0, kt, c0:c0 + w], TMP[:, b, c0:c0 + w], ACT.Identity,
                                               bias=MOD[:, l, q, bass.ds(shift * KT + kt, 1)])
                ins.then_inc(s["hi"], 1)
            with act.Fori(0, KT // 2) as j:
                for b in range(2):
                    tile(2 * j + b, b)

        act.wait_ge(vec_T, 1)
        copy(VEC[:, :], PS[4][:, 0:S_COL + 56]).then_inc(vec_ready, 1)
        act.wait_ge(vec_ready, 1)
        act.wait_ge(sil_zero, 1)
        for q in range(2):
            v = VEC[:, S_COL + (1 - q) * KT:S_COL + (2 - q) * KT]
            nc.scalar.activation(SIL[:, :, q], v, ACT.Silu).then_inc(sil_ready, 1)
        for n in range(8):
            act.wait_ge(tok_T, n + 1)
            k = (n % 2) * 8
            copy(H[:, k:k + 4, (n // 2) * P:(n // 2 + 1) * P],
                 PS[2 * (n % 2)][:, :].rearrange("p (k t) -> p k t", k=4)).then_inc(tok_a, 1)
        act.wait_ge(tok_a, 8)
        act.wait_ge(tok_b, 8)
        squares(n0, lambda kt: H[:, kt, :], None, TOK)
        root(n0, TOK)

        def ada_evac(n, bank, row, rt=0):
            act.wait_ge(raw_done[n % RAW_SLOTS], n // RAW_SLOTS + 1 + rt)
            copy(row, bank[:, :]).then_inc(ada_row, 1)

        act.wait_ge(n0["std"], n0["one0"] + 1)
        for b in range(2):
            ada_evac(N_ADA0 + (b + 1) * ADA_U - 1, PS[b], SQ[:, b, :])

        def evac_pair(j, first_chunk):
            for b in range(2):
                chunk = first_chunk + 2 * j + b
                act.wait_ge(sel_done, chunk - 1)
                ada_evac(N_ADA0 + (first_chunk + b + 1) * ADA_U - 1, PS[b], SQ[:, b, :], j * (2 * ADA_U // RAW_SLOTS))

        with act.Fori(0, 3) as j:
            evac_pair(j, 2)
        with act.Fori(0, KT // 2) as j:
            for b in range(2):
                kt = 2 * j + b
                act.wait_ge(sel_done, 8 + kt - 1)
                ada_evac(N_ADA0 + (9 + b) * ADA_U - 1, PS[b], SQ[:, b, :], j * (2 * ADA_U // RAW_SLOTS))
                act.wait_ge(pool["t"], kt + 1)
                act.wait_ge(pool["d"], kt + 1)
                for q, c0, w in both:
                    ins = nc.scalar.activation(PU[:, q, PAD:PAD + w], TMP[:, 0, c0:c0 + w], ACT.Identity,
                                               bias=MOD[:, 0, q, bass.ds(kt, 1)])
                ins.then_inc(pool["u"], 1)
                act.wait_ge(pool["d"], kt + 2)
                copy(U[:, 0, kt, :], PD[:, :]).then_inc(pool["hi"], 1)
        for k in range(4):
            split_hi(N_POOL + k, M_POOL + k)
        for u in range(8):
            if u < 4:
                split_hi(N_POOL + 4 + u, M_POOL + 4 + u)
            if u % 2 == 1:
                act.wait_ge(mult_done, M_POOL + u + 1)
                g = u // 2
                for t in range(4):
                    kt = 4 * g + t
                    nc.scalar.activation(Y[:, kt, :], PS[4 * (g % 2) + t][:, :], ACT.Copy,
                                         scale=VEC[:, PS_COL + kt:PS_COL + kt + 1]).then_inc(pool["y"], 1)

        def prime(n, m):
            for k in range(RAW_SLOTS):
                split_hi(n + k, m + k)

        def prime_ffn(l, n, m, late=False):
            early = RAW_SLOTS - (1 if l == 0 else 0)
            for t in range(early, RAW_SLOTS) if late else range(early):
                split_hi(n + ffn_place(l, t), m + t)

        def run_ffn(l, n_base, m_base, nt):
            s = ffn[l]
            step = ffn_units(l)

            def iteration(n, m, i, slot, rt=0, mt=0, up_only=False, last=False):
                for t in range(W_U):
                    split_hi(n + ffn_ahead(l, t, up_only), m + t + 4, rt, mt)
                act.wait_ge(s["lo"], 2 * i)
                act.wait_ge(mult_done, m + W_U + mt * RAW_SLOTS)
                for a in range(2):
                    nc.scalar.activation(SQ[:, a, 0:nt], PS[a][:, 0:nt], ACT.Silu).then_inc(s["silu"], 1)
                late = 1 if up_only else 0
                for t in range(W_U, 2 * W_U - late):
                    split_hi(n + ffn_ahead(l, t, up_only), m + t + 4, rt, mt)
                if l == 0:
                    act.wait_ge(mod_ready, 2 * (CHUNKS + i))
                    ada_evac(n + ffn_place(l, 2 * W_U - 1) + 1, PS[4], ACC[:, :], rt)
                for a in range(2):
                    act.wait_ge(s["hf"], 2 * i + a + 1)
                    copy(HC[:, slot, 0, a, 0:nt], SQ[:, a, 0:nt]).then_inc(s["hi"], 1)
                for t in range(2 * W_U - late, 2 * W_U + (0 if up_only else W2_U)):
                    split_hi(n + ffn_ahead(l, t, up_only, last), m + t + 4, rt, mt)

            prime_ffn(l, n_base, m_base, late=True)
            iteration(n_base, m_base, 0, 0, up_only=True)
            n, m = n_base + step - W2_U, m_base + 8
            with act.Fori(0, (FFN_IT - 2) // 2) as j:
                for b in range(2):
                    iteration(n + b * step, m + 12 * b, 2 * j + 1 + b, 1 - b, j * (2 * step // RAW_SLOTS), j * 6)
            iteration(n + (FFN_IT - 2) * step, m + (FFN_IT - 2) * 12, FFN_IT - 1, 1, last=True)

        prime_ffn(0, N_FFN0, M_FFN0)
        act.wait_ge(mod_ready, 2 * CHUNKS)
        squares(norm01, lambda kt: Y[:, kt, :], pool["y"], TOK)
        root(norm01, TOK)
        act.wait_ge(norm01["rstd"], norm01["one0"] + 1)
        squares(norm02, lambda kt: H[:, kt, :], norm01["h"], TOK)
        root(norm02, TOK)
        apply_hi(norm02, 0, 3, both)
        run_ffn(0, N_FFN0, M_FFN0, TOK)
        for k in range(CHUNKS - ADA_LOOPED):
            act.wait_ge(mod_ready, 2 * (CHUNKS + ADA_LOOPED + k))
            ada_evac(N_ADA1 + (k + 1) * ADA_U - 1, PS[4], ACC[:, :])
        prime(N_DQKV, M_DQKV)
        act.wait_ge(ffn[0]["y_free"], 4 + 16 * FFN_IT)
        act.wait_ge(mod_ready, 4 * CHUNKS)
        squares(norm03, lambda kt: Y[:, kt, :], None, TOK)
        root(norm03, TOK)
        act.wait_ge(norm03["rstd"], norm03["one0"] + 1)
        squares(norm10, lambda kt: H[:, kt, :], norm03["h"], TOK)
        root(norm10, TOK)
        apply_hi(norm10, 1, 0, both)

        for pr in range(4):
            for u in range(4):
                k = 4 * pr + u + 4
                if k < DQKV_U:
                    split_hi(N_DQKV + k, M_DQKV + k)
            act.wait_ge(mult_done, M_DQKV + 4 * pr + 4)
            for a in range(2):
                dst = CQ[:, 2 * pr + a, :] if pr < 2 else CKV[:, 2 * pr - 4 + a, :]
                nt = SEQ if pr < 2 else TOK
                copy(dst, PS[2 * pr + a][:, 0:nt]).then_inc(dq["evac"], 1)
        act.wait_ge(dq["evac"], 8)
        nc.scalar.activation(LSQ_Q[:, :, :], CQ[:, :, :], ACT.Square).then_inc(dq["sq"], 1)
        nc.scalar.activation(LSQ_KV[:, :, :], CKV[:, :, :], ACT.Square).then_inc(dq["sq"], 1)
        act.wait_ge(mult_done, M_DQKV + DQKV_U)
        copy(KRAW[:, :], PS[0][:, :]).then_inc(dq["evac"], 1)
        act.wait_ge(dq["var"], 2)
        nc.scalar.activation(RSTDQ[:, :], RSTDQ[:, :], ACT.Sqrt).then_inc(dq["std"], 1)
        nc.scalar.activation(RSTD[:, :], ACC[:, :], ACT.Sqrt).then_inc(dq["std"], 1)
        for k in range(LT):
            act.wait_ge(dq["t"], k + 1)
            copy(QL[:, 0, k, :], CQ[:, k, :]).then_inc(dq["hi"], 1)
        for k in range(LT):
            act.wait_ge(dq["t"], LT + k + 1)
            copy(KVL[:, 0, k, :], CKV[:, k, :]).then_inc(dq["hi"], 1)
        act.wait_ge(dq["rot"], 1)
        copy(KR[:, 0, 0:CTX], KRAW[:, 0:CTX])
        copy(KR[:, 0, CTX:TOK], KROT[:, :]).then_inc(dq["krhi"], 1)
        for u in range(4):
            split_hi(N_HEADS + u, M_HEADS + u)

        def next_unit(pair, u, rt, mt, m, last):
            if not last:
                k = 4 + u + (m - M_HEADS)
                split_hi(N_HEADS + k, M_HEADS + k, rt, mt)

        def head_project(pair, m, vslot, rt=0, mt=0, last=False):
            act.wait_ge(mult_done, m + 2 + mt * RAW_SLOTS)
            if not (isinstance(pair, int) and pair == 0):
                act.wait_ge(hd["s"], 4 * pair)
                act.wait_ge(hd["qr_lo"], pair)
            copy(QN[:, 0, :, :], PS[0][:, :].rearrange("p (h q) -> p h q", h=2)).then_inc(hd["qn_hi"], 1)
            copy(QF[:, :], PS[1][:, 0:SEQ]).then_inc(hd["qf"], 1)
            next_unit(pair, 0, rt, mt, m, last)
            next_unit(pair, 1, rt, mt, m, last)
            for a in range(2):
                act.wait_ge(hd["kpe"], 2 * pair + a + 1)
                copy(KN[:, 0, a, :], PS[2][:, :]).then_inc(hd["kn_hi"], 1)
                act.wait_ge(mult_done, m + 3 + a + mt * RAW_SLOTS)
                copy(V[:, vslot, 0, a, :], PS[3][:, :]).then_inc(hd["v_hi"], 1)
                next_unit(pair, 2 + a, rt, mt, m, last)
                if a == 0:
                    act.wait_ge(hd["rot"], pair + 1)
                    copy(QR[0:ROPE, 0, 0, :], QF[0:ROPE, :])
                    copy(QR[ROPE:P, 0, 1, :], QF[ROPE:P, :]).then_inc(hd["qr_hi"], 1)

        def exps(pair, a):
            for qt in range(2):
                k = 4 * pair + 2 * a + qt
                act.wait_ge(hd["nmax"], k + 1)
                if not (isinstance(pair, int) and pair == 0):
                    act.wait_ge(hd["pt"], k - 3)
                nc.scalar.activation(PR[:, a, qt, :], PS[4 + qt][:, :], ACT.Exp, bias=SMALL[:, 1, 2 * a + qt:2 * a + qt + 1],
                                     scale=SCALE, accum_out=SMALL[:, 2, 2 * a + qt:2 * a + qt + 1]).then_inc(hd["exp"], 1)

        def weigh_hi(pair, a):
            h = 2 * pair + a
            for qt in range(2):
                act.wait_ge(hd["pt"], 2 * h + qt + 1)
                if not (isinstance(pair, int) and pair == 0 and a == 0):
                    act.wait_ge(hd["o"], h)
                copy(PT[:, 0, :, qt * P:(qt + 1) * P],
                     PS[6 + qt][:, :].rearrange("p (j q) -> p j q", j=4)).then_inc(hd["pt_hi"], 1)

        def out_hi(pair, a):
            h = 2 * pair + a
            act.wait_ge(hd["o"], h + 1)
            dst = OT[:, 0, h, :] if isinstance(h, int) else OT[:, 0, bass.ds(h, 1), :].rearrange("p a q -> p (a q)")
            copy(dst, PS[1][:, a * SEQ:(a + 1) * SEQ]).then_inc(hd["o_hi"], 1)

        def head_pair(pair, m, vslot, rt=0, mt=0, last=False):
            head_project(pair, m, vslot, rt, mt, last)
            for a in range(2):
                weigh_hi(pair - 1, a)
                out_hi(pair - 1, a)
                exps(pair, a)

        head_project(0, M_HEADS, 0)
        exps(0, 0)
        exps(0, 1)
        head_pair(1, M_HEADS + 4, 1)
        with act.Fori(0, 2) as j:
            for b in range(2):
                head_pair(2 * j + 2 + b, M_HEADS + 8 + 4 * b, b, j * 2, j * 2)
        head_pair(6, M_HEADS + 24, 0)
        head_pair(7, M_HEADS + 28, 1, last=True)
        for u in range(4):
            split_hi(N_WO + u, M_WO + u)
        for a in range(2):
            weigh_hi(HEADS // 2 - 1, a)
            out_hi(HEADS // 2 - 1, a)

        def out_evac(dp, m, bank, mt=0):
            act.wait_ge(mult_done, m + 4 + mt * RAW_SLOTS)
            for a in range(2):
                kt = 2 * dp + a
                copy(Y1[:, kt, :], PS[bank + a][:, 0:SEQ]).then_inc(wo_y, 1)

        act.wait_ge(hd["pt_lo"], 2 * HEADS)
        with act.Fori(0, 3) as j:
            for b in range(2):
                for u in range(4):
                    split_hi(N_WO + 4 + 4 * b + u, M_WO + 4 + 4 * b + u, j * 2, j * 2)
                out_evac(2 * j + b, M_WO + 4 * b, 2 + 2 * b, j * 2)
        for u in range(4):
            split_hi(N_WO + 28 + u, M_WO + 28 + u)
        out_evac(6, M_WO + 24, 2)
        out_evac(7, M_WO + 28, 4)

        prime_ffn(1, N_FFN1, M_FFN1)
        squares(norm11, lambda kt: Y1[:, kt, :], wo_y, SEQ)
        root(norm11, SEQ)
        act.wait_ge(norm11["rstd"], norm11["one0"] + 1)
        squares(norm12, lambda kt: H[:, kt, CTX:TOK], norm11["h"], SEQ)
        root(norm12, SEQ)
        apply_hi(norm12, 1, 3, latent)
        run_ffn(1, N_FFN1, M_FFN1, SEQ)
        act.wait_ge(ffn[1]["y_free"], 4 + 16 * FFN_IT)
        squares(norm13, lambda kt: Y[:, kt, 0:SEQ], None, SEQ)
        root(norm13, SEQ)
        for t in range(2):
            for q in (0, 2):
                act.wait_ge(out_T, 4 * t + q + 1)
                copy(OUTT[:, t, 512 * q:512 * q + 512], PS[4 * t + q][:, :]).then_inc(out_a, 1)

    @block.vector
    def _(dve):
        def split_lo(n, m, rt=0, mt=0):
            dve.wait_ge(hi_ready, m + 1 + mt * RAW_SLOTS)
            for raw, split in unit_parts(n, m):
                ins = nc.vector.tensor_tensor(split(1), raw, split(0).bitcast(F32), ALU.subtract)
            ins.then_inc(raw_done[n % RAW_SLOTS], 1)

        def low(dst, src, hi):
            return nc.vector.tensor_tensor(dst, src, hi.bitcast(F32), ALU.subtract)

        def add_squares(s, n_tok):
            nc.vector.memset(ACC[:, 0:n_tok], 0.0).then_inc(s["acc"], 2)
            with dve.Fori(0, KT // 2) as j:
                for b in range(2):
                    kt = 2 * j + b
                    dve.wait_ge(s["sq"], s["sq0"] + kt + 1)
                    dve.wait_ge(s["acc"], s["acc0"] + kt + 2)
                    nc.vector.tensor_tensor(ACC[:, 0:n_tok], ACC[:, 0:n_tok], SQ[:, b, 0:n_tok], ALU.add).then_inc(s["acc"], 1)

        def reciprocal_root(s, n_tok):
            dve.wait_ge(s["ss"], s["one0"] + 1)
            nc.vector.tensor_scalar(ACC[:, 0:n_tok], PS[7][:, 0:n_tok], 1.0 / D, EPS, ALU.mult, ALU.add).then_inc(s["var"], 1)
            dve.wait_ge(s["std"], s["one0"] + 1)
            nc.vector.reciprocal(RSTD[:, 0:n_tok], RSTD[:, 0:n_tok]).then_inc(s["rstd"], 1)
            dve.wait_ge(s["rstd"], s["one0"] + 1)

        def update(s, src, col, segs, c0, n_tok):
            def product(kt, b, waits=True):
                if waits:
                    dve.wait_ge(s["h"], kt - 1)
                for q, t0, w in segs:
                    o = t0 - c0
                    ins = nc.vector.scalar_tensor_tensor(TMP[:, b, o:o + w], src(kt, o, w), COL[:, col, q, bass.ds(kt, 1)],
                                                         RSTD[:, o:o + w], ALU.mult, ALU.mult)
                ins.then_inc(s["t"], 1)

            def add(kt, b):
                dve.wait_ge(s["t"], kt + 1)
                nc.vector.tensor_tensor(H[:, kt, c0:c0 + n_tok], H[:, kt, c0:c0 + n_tok], TMP[:, b, 0:n_tok],
                                        ALU.add).then_inc(s["h"], 1)

            product(0, 0, waits=False)
            product(1, 1, waits=False)
            add(0, 0)
            with dve.Fori(0, KT // 2 - 1) as j:
                for b in range(2):
                    product(2 * j + 2 + b, b)
                    add(2 * j + 1 + b, 1 - b)
            add(KT - 1, 1)

        def apply(s, l, shift, col, segs, c0):
            def product(kt, b, waits=True):
                if waits:
                    dve.wait_ge(s["lo"], kt - 1)
                for q, t0, w in segs:
                    ins = nc.vector.scalar_tensor_tensor(TMP[:, b, t0:t0 + w], H[:, kt, t0:t0 + w],
                                                         COL[:, col, q, bass.ds(kt, 1)],
                                                         RSTD[:, t0 - c0:t0 - c0 + w], ALU.mult, ALU.mult)
                ins.then_inc(s["t"], 1)

            def lo(kt, b):
                dve.wait_ge(s["hi"], kt + 1)
                for q, t0, w in segs:
                    ins = nc.vector.scalar_tensor_tensor(U[:, 1, kt, t0:t0 + w], TMP[:, b, t0:t0 + w],
                                                         MOD[:, l, q, bass.ds(shift * KT + kt, 1)],
                                                         U[:, 0, kt, t0:t0 + w].bitcast(F32), ALU.add, ALU.subtract)
                ins.then_inc(s["lo"], 1)

            product(0, 0, waits=False)
            product(1, 1, waits=False)
            lo(0, 0)
            with dve.Fori(0, KT // 2 - 1) as j:
                for b in range(2):
                    product(2 * j + 2 + b, b)
                    lo(2 * j + 1 + b, 1 - b)
            lo(KT - 1, 1)

        def mod_columns(l, chunk, ct, bank):
            dve.wait_ge(sel_done, chunk + 1)
            for q in range(2):
                nc.vector.tensor_tensor(MOD[:, l, q, bass.ds(ct * 4, 4)], bank[:, q:8:2],
                                        VEC[:, bass.ds(B_COL + 96 * l + ct * 4, 4)], ALU.add).then_inc(mod_ready, 1)

        def scale_gate(l, part):
            for q in range(2):
                j = (1, 2, 4, 5)[part]
                src = MOD[:, l, q, j * KT:(j + 1) * KT]
                g = VEC[:, G_COL + (4 * l + part) * KT:G_COL + (4 * l + part + 1) * KT]
                if part % 2 == 0:
                    ins = nc.vector.scalar_tensor_tensor(COL[:, 4 * l + part, q, :], src, 1.0, g, ALU.add, ALU.mult)
                else:
                    ins = nc.vector.tensor_tensor(COL[:, 4 * l + part, q, :], src, g, ALU.mult)
            ins.then_inc(col_ready, 1)
            dve.wait_ge(col_ready, 4 * l + part + 1)

        for n in range(8):
            dve.wait_ge(raw_done[n % RAW_SLOTS], n // RAW_SLOTS + 1)
            k = (n % 2) * 8 + 4
            nc.vector.tensor_copy(H[:, k:k + 4, (n // 2) * P:(n // 2 + 1) * P],
                                  PS[2 * (n % 2) + 1][:, :].rearrange("p (k t) -> p k t", k=4)).then_inc(tok_b, 1)
        add_squares(n0, TOK)
        reciprocal_root(n0, TOK)
        dve.wait_ge(vec_ready, 1)
        with dve.Fori(0, 4) as j:
            for b in range(2):
                mod_columns(0, 2 * j + b, 2 * j + b, PS[2 + b])
        dve.wait_ge(mod_ready, 16)
        scale_gate(0, 0)
        dve.wait_ge(pinv_in, 16)

        def pooled_tile(kt, g):
            for q, t0, w in both:
                ins = nc.vector.scalar_tensor_tensor(TMP[:, 0, t0:t0 + w], H[:, kt, t0:t0 + w],
                                                     COL[:, 0, q, bass.ds(kt, 1)], RSTD[:, t0:t0 + w],
                                                     ALU.mult, ALU.mult)
            ins.then_inc(pool["t"], 1)
            dve.wait_ge(pool["s"], kt + 1)
            total = (PA, PB, PA, PB)[g]
            for q in range(2):
                ins = nc.vector.tensor_tensor(PD[:, q * SEQ:(q + 1) * SEQ], total[:, q, PAD:PAD + SEQ],
                                              PINV[:, g, :], ALU.mult)
            ins.then_inc(pool["m"], 1)
            dve.wait_ge(pool["m"], kt + 1)
            by_seq = PD[:, :].rearrange("p (q t) -> p q t", q=2)
            nc.vector.tensor_tensor(by_seq, by_seq, PU[:, :, PAD:PAD + SEQ], ALU.subtract).then_inc(pool["d"], 1)
            dve.wait_ge(pool["d"], kt + 2)
            dve.wait_ge(pool["hi"], kt + 1)
            low(U[:, 1, kt, :], PD[:, :], U[:, 0, kt, :]).then_inc(pool["lo"], 1)

        for g in range(4):
            with dve.Fori(0, 2) as j:
                for b in range(2):
                    kt = 2 * j + 4 * g + b
                    pooled_tile(kt, g)
                    mod_columns(0, 8 + kt, 8 + kt, PS[2 + b])
                    dve.wait_ge(pool["lo"], kt + 1)

        def prime(n, m):
            for k in range(RAW_SLOTS):
                split_lo(n + k, m + k)

        def prime_ffn(l, n, m, late=False):
            early = RAW_SLOTS - (1 if l == 0 else 0)
            for t in range(early, RAW_SLOTS) if late else range(early):
                split_lo(n + ffn_place(l, t), m + t)

        prime(N_POOL, M_POOL)
        for k in range(4):
            split_lo(N_POOL + 4 + k, M_POOL + 4 + k)
        dve.wait_ge(mod_ready, 2 * CHUNKS)
        for part in range(1, 4):
            scale_gate(0, part)

        def run_ffn(l, n_base, m_base, nt):
            s = ffn[l]
            step = ffn_units(l)

            def hidden(m, i, mt):
                for a in range(2):
                    dve.wait_ge(s["silu"], 2 * i + a + 1)
                    dve.wait_ge(mult_done, m + 2 * W_U + mt * RAW_SLOTS)
                    nc.vector.tensor_tensor(SQ[:, a, 0:nt], SQ[:, a, 0:nt], PS[2 + a][:, 0:nt],
                                            ALU.mult).then_inc(s["hf"], 1)

            def hidden_lo(i, slot):
                for a in range(2):
                    dve.wait_ge(s["hf"], 2 * i + a + 1)
                    dve.wait_ge(s["hi"], 2 * i + a + 1)
                    low(HC[:, slot, 1, a, 0:nt], SQ[:, a, 0:nt], HC[:, slot, 0, a, 0:nt]).then_inc(s["lo"], 1)

            def up(n, m, i, rt=0, mt=0, up_only=False):
                for t in range(2 * W_U - (1 if up_only else 0)):
                    split_lo(n + ffn_ahead(l, t, up_only), m + t + 4, rt, mt)
                hidden(m, i, mt)
                if l == 0:
                    mod_columns(1, CHUNKS + i, i, PS[5])

            def add_down(m, i, u, mt=0):
                for b in range(4):
                    if b < 3:
                        dve.wait_ge(s["y"], 3 * (4 * i + u) + b + 1)
                    else:
                        dve.wait_ge(mult_done, m + 1 + mt * RAW_SLOTS)
                    kt = 4 * u + b
                    nc.vector.tensor_tensor(Y[:, kt, 0:nt], Y[:, kt, 0:nt], PS[4 + b][:, 0:nt],
                                            ALU.add).then_inc(s["y_free"], 1)

            def iteration(n, m, i, slot, rt=0, mt=0, last=False):
                up(n, m, i, rt, mt)
                dve.wait_ge(s["y_free"], 4 + 16 * (i - 1))
                for u in range(W2_U):
                    add_down(m + 2 * W_U + u, i - 1, u, mt)
                    if u == 0:
                        hidden_lo(i, slot)
                    split_lo(n + ffn_ahead(l, 2 * W_U + u, False, last), m + 2 * W_U + u + 4, rt, mt)

            prime_ffn(l, n_base, m_base, late=True)
            up(n_base, m_base, 0, up_only=True)
            hidden_lo(0, 0)
            split_lo(n_base + ffn_ahead(l, 2 * W_U - 1, True), m_base + 2 * W_U + 3)
            n, m = n_base + step - W2_U, m_base + 8
            with dve.Fori(0, (FFN_IT - 2) // 2) as j:
                for b in range(2):
                    iteration(n + b * step, m + 12 * b, 2 * j + 1 + b, 1 - b, j * (2 * step // RAW_SLOTS), j * 6)
            n, m = n + (FFN_IT - 2) * step, m + (FFN_IT - 2) * 12
            iteration(n, m, FFN_IT - 1, 1, last=True)
            dve.wait_ge(s["y_free"], 4 + 16 * (FFN_IT - 1))
            for u in range(W2_U):
                add_down(m + 12 + u, FFN_IT - 1, u)

        prime_ffn(0, N_FFN0, M_FFN0)
        add_squares(norm01, TOK)
        reciprocal_root(norm01, TOK)
        update(norm01, lambda kt, o, w: Y[:, kt, o:o + w], 1, both, 0, TOK)
        reciprocal_root(norm02, TOK)
        apply(norm02, 0, 3, 2, both, 0)
        run_ffn(0, N_FFN0, M_FFN0, TOK)
        for k in range(CHUNKS - ADA_LOOPED):
            mod_columns(1, CHUNKS + ADA_LOOPED + k, ADA_LOOPED + k, PS[5])
        prime(N_DQKV, M_DQKV)
        dve.wait_ge(mod_ready, 4 * CHUNKS)
        for part in range(4):
            scale_gate(1, part)
        add_squares(norm03, TOK)
        reciprocal_root(norm03, TOK)
        update(norm03, lambda kt, o, w: Y[:, kt, o:o + w], 3, both, 0, TOK)
        reciprocal_root(norm10, TOK)
        apply(norm10, 1, 0, 4, both, 0)

        for k in range(4, DQKV_U):
            split_lo(N_DQKV + k, M_DQKV + k)
        dve.wait_ge(dq["ss"], 1)
        nc.vector.tensor_scalar(RSTDQ[:, :], PS[2][:, 0:SEQ], 1.0 / LORA, EPS, ALU.mult, ALU.add).then_inc(dq["var"], 1)
        nc.vector.tensor_scalar(ACC[:, :], PS[3][:, :], 1.0 / LORA, EPS, ALU.mult, ALU.add).then_inc(dq["var"], 1)
        dve.wait_ge(dq["std"], 2)
        nc.vector.reciprocal(RSTDQ[:, :], RSTDQ[:, :]).then_inc(dq["rstd"], 1)
        nc.vector.reciprocal(RSTD[:, :], RSTD[:, :]).then_inc(dq["rstd"], 1)
        dve.wait_ge(dq["rstd"], 2)
        for k in range(2 * LT):
            kind, i = divmod(k, LT)
            lat, r, g = ((CQ, RSTDQ, QN_COL), (CKV, RSTD, KVN_COL))[kind]
            nc.vector.scalar_tensor_tensor(lat[:, i, :], lat[:, i, :], VEC[:, g + i:g + i + 1], r[:, :],
                                           ALU.mult, ALU.mult).then_inc(dq["t"], 1)
        for k in range(2 * LT):
            kind, i = divmod(k, LT)
            lat, dst = ((CQ, QL), (CKV, KVL))[kind]
            dve.wait_ge(dq["t"], k + 1)
            dve.wait_ge(dq["hi"], k + 1)
            low(dst[:, 1, i, :], lat[:, i, :], dst[:, 0, i, :]).then_inc(dq["lo"], 1)
        dve.wait_ge(tables_in, 32)
        dve.wait_ge(dq["swap"], 1)
        nc.vector.tensor_tensor(KSIN[:, :], SIN, PS[4][:, 0:SEQ], ALU.mult).then_inc(dq["sin"], 1)
        nc.vector.tensor_tensor(KROT[:, :], COS, KRAW[:, CTX:TOK], ALU.mult).then_inc(dq["cos"], 1)
        dve.wait_ge(dq["sin"], 1)
        dve.wait_ge(dq["cos"], 1)
        nc.vector.tensor_tensor(KROT[:, :], KROT[:, :], KSIN[:, :], ALU.add).then_inc(dq["rot"], 1)
        dve.wait_ge(dq["rot"], 1)
        dve.wait_ge(dq["krhi"], 1)
        low(KR[:, 1, 0:CTX], KRAW[:, 0:CTX], KR[:, 0, 0:CTX])
        low(KR[:, 1, CTX:TOK], KROT[:, :], KR[:, 0, CTX:TOK]).then_inc(dq["krlo"], 1)
        for u in range(4):
            split_lo(N_HEADS + u, M_HEADS + u)

        def next_unit(u, rt, mt, m, last):
            if not last:
                k = 4 + u + (m - M_HEADS)
                split_lo(N_HEADS + k, M_HEADS + k, rt, mt)

        def head_project(pair, m, vslot, rt=0, mt=0, last=False):
            dve.wait_ge(hd["qn_hi"], pair + 1)
            low(QN[:, 1, :, :], PS[0][:, :].rearrange("p (h q) -> p h q", h=2), QN[:, 0, :, :]).then_inc(hd["qn_lo"], 1)
            next_unit(0, rt, mt, m, last)
            next_unit(1, rt, mt, m, last)
            for a in range(2):
                dve.wait_ge(hd["kn_hi"], 2 * pair + a + 1)
                low(KN[:, 1, a, :], PS[2][:, :], KN[:, 0, a, :]).then_inc(hd["kn_lo"], 1)
                dve.wait_ge(hd["v_hi"], 2 * pair + a + 1)
                low(V[:, vslot, 1, a, :], PS[3][:, :], V[:, vslot, 0, a, :]).then_inc(hd["v_lo"], 1)
                if a == 0:
                    dve.wait_ge(hd["swap"], pair + 1)
                    nc.vector.tensor_tensor(QS[:, :], SIN, PS[1][:, SEQ:2 * SEQ], ALU.mult).then_inc(hd["sin"], 1)
                    nc.vector.tensor_tensor(QF[:, :], COS, QF[:, :], ALU.mult).then_inc(hd["cos"], 1)
                    dve.wait_ge(hd["sin"], pair + 1)
                    dve.wait_ge(hd["cos"], pair + 1)
                    nc.vector.tensor_tensor(QF[:, :], QF[:, :], QS[:, :], ALU.add).then_inc(hd["rot"], 1)
                next_unit(2 + a, rt, mt, m, last)
                if a == 1:
                    dve.wait_ge(hd["rot"], pair + 1)
                    dve.wait_ge(hd["qr_hi"], pair + 1)
                    low(QR[0:ROPE, 1, 0, :], QF[0:ROPE, :], QR[0:ROPE, 0, 0, :])
                    low(QR[ROPE:P, 1, 1, :], QF[ROPE:P, :], QR[ROPE:P, 0, 1, :]).then_inc(hd["qr_lo"], 1)

        def softmax(pair, a):
            for qt in range(2):
                k, col = 4 * pair + 2 * a + qt, 2 * a + qt
                dve.wait_ge(hd["s"], k + 1)
                nc.vector.reduce_max(SMALL[:, 0, col:col + 1], PS[4 + qt][:, :], AX.X).then_inc(hd["max"], 1)
                dve.wait_ge(hd["max"], k + 1)
                nc.vector.tensor_scalar(SMALL[:, 1, col:col + 1], SMALL[:, 0, col:col + 1], -SCALE, None,
                                        ALU.mult).then_inc(hd["nmax"], 1)
            for qt in range(2):
                k, col = 4 * pair + 2 * a + qt, 2 * a + qt
                dve.wait_ge(hd["exp"], k + 1)
                nc.vector.reciprocal(SMALL[:, 3, col:col + 1], SMALL[:, 2, col:col + 1]).then_inc(hd["rinv"], 1)
                dve.wait_ge(hd["rinv"], k + 1)
                nc.vector.tensor_scalar(PR[:, a, qt, :], PR[:, a, qt, :], SMALL[:, 3, col:col + 1], None,
                                        ALU.mult).then_inc(hd["p"], 1)

        def weigh_lo(pair, a):
            h = 2 * pair + a
            for qt in range(2):
                dve.wait_ge(hd["pt_hi"], 2 * h + qt + 1)
                q = slice(qt * P, (qt + 1) * P)
                low(PT[:, 1, :, q], PS[6 + qt][:, :].rearrange("p (j q) -> p j q", j=4), PT[:, 0, :, q]).then_inc(hd["pt_lo"], 1)
            dve.wait_ge(hd["o_hi"], h + 1)
            low(OT[:, 1, h, :], PS[1][:, a * SEQ:(a + 1) * SEQ], OT[:, 0, h, :]).then_inc(hd["o_lo"], 1)

        def head_pair(pair, m, vslot, rt=0, mt=0, last=False):
            head_project(pair, m, vslot, rt, mt, last)
            for a in range(2):
                weigh_lo(pair - 1, a)
                softmax(pair, a)

        head_project(0, M_HEADS, 0)
        softmax(0, 0)
        softmax(0, 1)
        head_pair(1, M_HEADS + 4, 1)
        with dve.Fori(0, 2) as j:
            for b in range(2):
                head_pair(2 * j + 2 + b, M_HEADS + 8 + 4 * b, b, j * 2, j * 2)
        head_pair(6, M_HEADS + 24, 0)
        head_pair(7, M_HEADS + 28, 1, last=True)
        prime(N_WO, M_WO)
        for a in range(2):
            weigh_lo(HEADS // 2 - 1, a)
        with dve.Fori(0, 3) as j:
            for k in range(8):
                split_lo(N_WO + 4 + k, M_WO + 4 + k, j * 2, j * 2)
        for k in range(28, 32):
            split_lo(N_WO + k, M_WO + k)

        prime_ffn(1, N_FFN1, M_FFN1)
        add_squares(norm11, SEQ)
        reciprocal_root(norm11, SEQ)
        update(norm11, lambda kt, o, w: Y1[:, kt, o:o + w], 5, latent, CTX, SEQ)
        reciprocal_root(norm12, SEQ)
        apply(norm12, 1, 3, 6, latent, CTX)
        run_ffn(1, N_FFN1, M_FFN1, SEQ)
        add_squares(norm13, SEQ)
        reciprocal_root(norm13, SEQ)
        update(norm13, lambda kt, o, w: Y[:, kt, o:o + w], 7, latent, CTX, SEQ)
        for t in range(2):
            for q in (1, 3):
                dve.wait_ge(out_T, 4 * t + q + 1)
                nc.vector.tensor_copy(OUTT[:, t, 512 * q:512 * q + 512], PS[4 * t + q][:, :]).then_inc(out_b, 1)

    @block.gpsimd
    def _(gp):
        nc.gpsimd.memset(ONES[:, :], 1.0).then_inc(ones_ready, 1)
        nc.gpsimd.memset(SIL[:, :, :], 0.0).then_inc(sil_zero, 1)
        for buf in (PU, PA, PB):
            ins = nc.gpsimd.memset(buf[:, :, :], 0.0)
        ins.then_inc(pool["d"], 1)
        gp.wait_ge(pool["d"], 1)

        width = SEQ + 2 * PAD

        def window_sums(kt, g):
            gp.wait_ge(pool["u"], kt + 1)
            gp.wait_ge(pool["d"], kt + 1)
            lo, hi, src = 0, width, PU
            for step in range(g + 1):
                left, right = (1, 0) if step == 0 else (1 << (step - 1), 1 << (step - 1))
                lo, hi = lo + left, hi - right
                dst = (PA, PB)[step % 2]
                if step:
                    gp.wait_ge(pool["partial"], 2 * g * (g - 1) + (kt - 4 * g) * g + step)
                ins = nc.gpsimd.tensor_tensor(dst[:, :, lo:hi], src[:, :, lo - left:hi - left],
                                              src[:, :, lo + right:hi + right], ALU.add)
                ins.then_inc(pool["s"] if step == g else pool["partial"], 1)
                src = dst

        for g in range(4):
            with gp.Fori(0, 4) as j:
                window_sums(j + 4 * g, g)

        def add_squares(s, n_tok):
            nc.gpsimd.memset(ACC[:, 0:n_tok], 0.0).then_inc(s["acc"], 2)
            with gp.Fori(0, KT // 2) as j:
                for b in range(2):
                    kt = 2 * j + b
                    gp.wait_ge(s["sq"], s["sq0"] + kt + 1)
                    gp.wait_ge(s["acc"], s["acc0"] + kt + 2)
                    nc.gpsimd.tensor_tensor(ACC[:, 0:n_tok], ACC[:, 0:n_tok], SQ[:, b, 0:n_tok], ALU.add).then_inc(s["acc"], 1)

        gp.wait_ge(norm01["std"], norm01["one0"] + 1)
        add_squares(norm02, TOK)
        gp.wait_ge(norm01["t"], KT)
        nc.gpsimd.memset(Y[:, :, :], 0.0).then_inc(ffn[0]["y_free"], 4)
        gp.wait_ge(norm03["std"], norm03["one0"] + 1)
        add_squares(norm10, TOK)
        gp.wait_ge(mult_done, M_DQKV + DQKV_U)
        nc.gpsimd.memset(QR[ROPE:P, :, 0, :].bitcast(F32), 0.0).then_inc(hd["qr_zero"], 1)
        nc.gpsimd.memset(QR[0:ROPE, :, 1, :].bitcast(F32), 0.0).then_inc(hd["qr_zero"], 1)
        gp.wait_ge(norm11["std"], norm11["one0"] + 1)
        add_squares(norm12, SEQ)
        gp.wait_ge(mult_done, M_WO + 32)
        nc.gpsimd.memset(Y[:, :, 0:SEQ], 0.0).then_inc(ffn[1]["y_free"], 4)

    stack.close()


def shape_constants():
    mats = np.zeros((P, P + 2 + P), np.float32)
    mats[:, 0:P] = np.eye(P)
    for r in range(P):
        if r % 32 < 2:
            mats[r, P + r % 32] = 1.0
        if (r // 16) % 2 == 0:
            mats[r + 16, P + 2 + r] = -1.0
        else:
            mats[r - 16, P + 2 + r] = 1.0
    axis = ROPE // 2
    inv = (np.float32(ROPE_BASE) ** (-np.arange(0, axis, 2, dtype=np.float32) / np.float32(axis))).astype(np.float32)
    t = np.arange(SEQ)
    ang = [(t // GRID_W).astype(np.float32)[None] * inv[:, None], (t % GRID_W).astype(np.float32)[None] * inv[:, None]]
    ang = np.concatenate([ang[0], ang[0], ang[1], ang[1]] * 2)
    rope = np.concatenate([np.cos(ang), np.sin(ang)], axis=1).astype(np.float32)
    counts = [np.minimum(t + w // 2, SEQ) - np.maximum(t - w // 2, 0) for w in WINDOWS]
    inverse = np.tile((1.0 / np.concatenate(counts)).astype(np.float32), (P, 1))
    return {"mats": mats, "rope_tables": rope, "pool_inv": inverse}


_INS = ["x", "ctx", "c", "c_ctx", "ada_w", "ada_b", "norm_g", "pool_w", "pool_scale", "mla_w_dqkv", "mla_q_norm",
        "mla_w_uq", "mla_kv_norm", "mla_w_ukv", "mla_w_o", "ffn_w1", "ffn_w3", "ffn_w2"]


def kernel(**inputs):
    import concourse.bacc as bacc
    from concourse.bass_utils import run_bass_kernel_spmd

    nc = bacc.Bacc("TRN2", target_bir_lowering=False, num_devices=1)
    arrays, args = {}, []
    for name, a in [(k, inputs[k]) for k in _INS] + list(shape_constants().items()):
        arrays["in_" + name] = np.ascontiguousarray(a)
        args.append(nc.dram_tensor("in_" + name, arrays["in_" + name].shape, F32, kind="ExternalInput").ap())
    out = nc.dram_tensor("out", (1, SEQ, D), F32, kind="ExternalOutput").ap()
    program(nc, *args, out)
    return run_bass_kernel_spmd(nc, [arrays], core_ids=[0]).results[0]["out"]
```

```python
from contextlib import ExitStack

import numpy as np

import concourse.bass as bass
from concourse import mybir

F32 = mybir.dt.float32
F32R = mybir.dt.float32r
ALU = mybir.AluOpType
ACT = mybir.ActivationFunctionType
AX = mybir.AxisListType

P = 128
D = 2048
KT = D // P
SEQ, CTX = 256, 256
TOK = CTX + SEQ
DFF = 5632
EPS = 1e-6
N_MOD = 6
HEADS, NOPE, ROPE, VD = 16, 128, 64, 128
LORA = 512
LT = LORA // P
QK = NOPE + ROPE
SCALE = float(QK) ** -0.5
WINDOWS = (2, 4, 8, 16)
PAD = max(WINDOWS) // 2
GRID_W = 64
ROPE_BASE = 10000.0

RAW_SLOTS = 4
UNIT = 1024
CHUNK = 512
CHUNKS = N_MOD * D // CHUNK
LATE = 2
ADA_U = KT * CHUNK // UNIT
FFN_IT = DFF // 256
W_U = KT * 256 // UNIT
W2_U = 2 * D // UNIT

N_TOK = 0
N_ADA0 = N_TOK + 8
N_POOL, M_POOL = N_ADA0 + (CHUNKS - LATE) * ADA_U, 0
N_LATE0 = N_POOL + 8
N_FFN0, M_FFN0 = N_LATE0 + LATE * ADA_U, M_POOL + 8
assert CHUNKS - LATE == FFN_IT
N_LATE1 = N_FFN0 + FFN_IT * (2 * W_U + W2_U + ADA_U)
N_DQKV, M_DQKV = N_LATE1 + LATE * ADA_U, M_FFN0 + FFN_IT * (2 * W_U + W2_U)
DQKV_U = 4 * 4 + 2
N_HEADS, M_HEADS = N_DQKV + DQKV_U, M_DQKV + DQKV_U
N_WO, M_WO = N_HEADS + 2 * HEADS, M_HEADS + 2 * HEADS
N_FFN1, M_FFN1 = N_WO + 32, M_WO + 32


def program(nc, x, ctx, c, c_ctx, ada_w, ada_b, norm_g, pool_w, pool_scale, w_dqkv, q_norm, w_uq,
            kv_norm, w_ukv, w_o, ffn_w1, ffn_w3, ffn_w2, mats, rope_tables, pool_inv, out):
    stack = ExitStack()

    def sem(name):
        return stack.enter_context(nc.semaphore(name))

    base = (nc.sbuf_base + 63) // 64 * 64

    def at(name, offset, shape, dt=F32):
        return nc.alloc_sbuf_tensor_at(name, [P] + shape, dt, offset=base + offset)

    KB = 1024
    Y_AT, H_AT, U_AT, HC_AT, RAW_AT, SPLIT_AT, MISC_AT = (k * KB for k in (0, 32, 64, 128, 144, 160, 192))
    Y = at("mixer_or_ffn_out", Y_AT, [KT, TOK])
    H = at("stream", H_AT, [KT, TOK])
    U = at("sublayer_in_hilo", U_AT, [2, KT, TOK], F32R)
    HC = at("ffn_hidden_hilo", HC_AT, [2, 2, 2, TOK], F32R)
    RAW = at("raw_units", RAW_AT, [RAW_SLOTS, UNIT])
    SPL = at("split_units", SPLIT_AT, [RAW_SLOTS, 2, UNIT], F32R)
    off = [MISC_AT]

    def misc(name, shape):
        t = at(name, off[0], shape)
        off[0] += (4 * int(np.prod(shape)) + 31) // 32 * 32
        return t

    MATS = misc("const_mats", [P + 2 + P])
    MOD = misc("mod_cols", [2, 2, N_MOD * KT])
    COL = misc("scale_gate_cols", [8, 2, KT])
    VEC = misc("param_cols", [P + 2 * 96 + 56])
    SIL = misc("silu_cols", [KT, 32])
    RSTD_AT = off[0]
    RSTD = misc("rstd", [TOK])
    ACC = misc("square_sum", [TOK])
    SQ = misc("squares", [2, TOK])
    SMALL = misc("softmax_cols", [4, 4])
    ONES = misc("ones", [P])
    assert base + off[0] <= nc.sbuf_usable_end, (off[0], nc.sbuf_usable_end)
    IDENT, SEL, SWAP = MATS[:, 0:P], MATS[:, P:P + 2], MATS[:, P + 2:P + 2 + P]
    G_COL, B_COL, S_COL = 0, P, P + 192
    PS_COL, QN_COL, KVN_COL = S_COL + 32, S_COL + 48, S_COL + 52
    ADA_ACC = at("ada_sums", RSTD_AT, [2, CHUNK])
    PINV = at("pool_inverse_counts", Y_AT + 28 * KB, [4, SEQ])
    ROWS = at("param_rows", HC_AT, [4, P])
    TMP = at("norm_tmp", HC_AT, [2, TOK])
    PU = at("pool_padded", HC_AT + 4 * KB, [2, SEQ + 2 * PAD])
    PA = at("pool_sum_a", HC_AT + 4 * KB + 2176, [2, SEQ + 2 * PAD])
    PB = at("pool_sum_b", HC_AT + 4 * KB + 2 * 2176, [2, SEQ + 2 * PAD])
    PD = at("pool_difference", HC_AT + 4 * KB + 3 * 2176, [TOK])
    CQ = at("q_latent", Y_AT, [LT, SEQ])
    CKV = at("kv_latent", Y_AT + 4 * KB, [LT, TOK])
    KRAW = at("k_rope_raw", Y_AT + 12 * KB, [TOK])
    LSQ_Q = at("q_latent_squares", Y_AT + 14 * KB, [LT, SEQ])
    LSQ_KV = at("kv_latent_squares", Y_AT + 18 * KB, [LT, TOK])
    KROT = at("k_rope_rotated", Y_AT + 26 * KB, [SEQ])
    KSIN = at("k_rope_sin_part", Y_AT + 27 * KB, [SEQ])
    RSTDQ = at("rstd_q", Y_AT + 28 * KB, [SEQ])
    OT = at("attn_out_hilo", Y_AT, [2, HEADS, SEQ], F32R)
    KVL = at("kv_latent_hilo", U_AT, [2, LT, TOK], F32R)
    QL = at("q_latent_hilo", U_AT + 16 * KB, [2, LT, SEQ], F32R)
    QN = at("q_nope_hilo", U_AT + 24 * KB, [2, 2, SEQ], F32R)
    QR = at("q_rope_hilo", U_AT + 28 * KB, [2, 2, SEQ], F32R)
    KN = at("k_nope_hilo", U_AT + 32 * KB, [2, 2, TOK], F32R)
    V = at("v_hilo", U_AT + 40 * KB, [2, 2, 2, TOK], F32R)
    PT = at("probs_T_hilo", U_AT + 56 * KB, [2, 4, SEQ], F32R)
    PTB = at("probs_T_hilo_b", H_AT, [KT, TOK], F32R)
    KR = at("k_rope_hilo", HC_AT, [2, TOK], F32R)
    PR = at("probs", HC_AT + 4 * KB, [2, 2, TOK])
    QF = at("q_rope_raw", HC_AT + 12 * KB, [SEQ])
    QS = at("q_rope_sin_part", HC_AT + 13 * KB, [SEQ])
    Y1 = at("attn_projected", U_AT + 48 * KB, [KT, SEQ])

    def probs_T(a, hl):
        return PT[:, hl, :, :] if a == 0 else PTB[:, 2 + 4 * hl:6 + 4 * hl, 0:SEQ]

    COS, SIN = H[:, 0, 0:SEQ], H[:, 1, 0:SEQ]
    OUTT = at("out_rows", U_AT, [2, D])

    PS = [stack.enter_context(nc.psum_tensor(f"bank{b}", [P, 512], F32)) for b in range(8)]

    raw_full = [sem(f"raw_full{s}") for s in range(RAW_SLOTS)]
    raw_done = [sem(f"raw_done{s}") for s in range(RAW_SLOTS)]
    hi_ready = sem("hi_ready")
    mult_done = sem("mult_done")
    consts_in, rows_in, tables_in, pinv_in = sem("consts_in"), sem("rows_in"), sem("tables_in"), sem("pinv_in")
    ones_ready, sil_zero = sem("ones_ready"), sem("sil_zero")
    vec_T, vec_ready, sil_ready = sem("vec_T"), sem("vec_ready"), sem("sil_ready")
    tok_T, tok_a, tok_b = sem("tok_T"), sem("tok_a"), sem("tok_b")
    ada_acc = sem("ada_acc")
    ada_row, sel_done, mod_ready = sem("ada_row"), sem("sel_done"), sem("mod_ready")
    col_ready = sem("col_ready")
    out_stored = sem("out_stored")

    def stage_sems(name, *parts):
        return {s: sem(f"{name}_{s}") for s in parts}

    stats = stage_sems("stats", "sq", "acc", "ss", "var", "std", "rstd")

    counted = {"norms": 0, "acc": 0, "ss": 0}

    def norm_stage(by_pe, *parts):
        k = counted["norms"]
        s = {p: sem(f"norm{k}_{p}") for p in parts}
        s.update(stats)
        s.update(by_pe=by_pe, sq0=k * KT, one0=k, acc0=counted["acc"], ss0=counted["ss"], ss1=KT if by_pe else 1)
        counted["norms"] += 1
        counted["acc"] += 0 if by_pe else KT + 2
        counted["ss"] += s["ss1"]
        return s

    n0 = norm_stage(False)
    norm01, norm02 = norm_stage(False, "t", "h"), norm_stage(True, "t", "hi", "lo")
    norm03, norm10 = norm_stage(False, "t", "h"), norm_stage(True, "t", "hi", "lo")
    norm11, norm12 = norm_stage(False, "t", "h"), norm_stage(True, "t", "hi", "lo")
    norm13 = norm_stage(False, "t", "h")
    norm02["after"], norm10["after"], norm12["after"] = norm01["h"], norm03["h"], norm11["h"]
    pool = {k: sem(f"pool_{k}") for k in ("t", "u", "partial", "s", "m", "d", "hi", "lo", "y")}
    ffn = [{k: sem(f"ffn{l}_{k}") for k in ("silu", "hf", "hi", "lo", "y", "y_free")} for l in range(2)]
    dq = {k: sem(f"dqkv_{k}") for k in ("evac", "sq", "ss", "var", "std", "rstd", "t", "hi", "lo",
                                        "swap", "sin", "cos", "rot", "krhi", "krlo")}
    hd = {k: sem(f"head_{k}") for k in ("qn_hi", "qn_lo", "qf", "swap", "sin", "cos", "rot", "qr_hi",
                                        "qr_lo", "kpe", "kn_hi", "kn_lo", "v_hi", "v_lo", "s", "max",
                                        "nmax", "exp", "rinv", "p", "pt", "pt_hi", "pt_lo", "o",
                                        "o_hi", "o_lo", "qr_zero")}
    wo_y = sem("wo_y")
    out_T, out_a, out_b = sem("out_T"), sem("out_a"), sem("out_b")

    block = stack.enter_context(nc.Block())

    both = [(0, 0, CTX), (1, CTX, SEQ)]
    latent = [(1, CTX, SEQ)]

    def ffn_units(l):
        return 2 * W_U + W2_U + (ADA_U if l == 0 else 0)

    def unit_parts(n, m):
        raw = RAW[:, n % RAW_SLOTS, :]
        slot = m % RAW_SLOTS
        if M_DQKV + 16 <= m < M_DQKV + DQKV_U:
            return [(raw[:, 0:8 * ROPE].rearrange("p (k r) -> p k r", k=8).unsqueeze(2).to_broadcast([P, 8, 2, ROPE]),
                     lambda hl: SPL[:, slot, hl, :].rearrange("p (k h r) -> p k h r", k=8, h=2))]
        if M_HEADS <= m < M_WO and (m - M_HEADS) % 4 < 2:
            cols = raw[:, 0:4 * QK].rearrange("p (k h q) -> p k h q", k=2, h=2)

            def split(hl, lo, hi):
                return SPL[:, slot, hl, 0:4 * QK].rearrange("p (k q) -> p k q", k=2)[:, :, lo:hi].rearrange(
                    "p k (h q) -> p k h q", h=2)

            return [(cols[:, :, :, 0:NOPE], lambda hl: split(hl, 0, 2 * NOPE)),
                    (cols[:, :, :, NOPE:QK], lambda hl: split(hl, 2 * NOPE, 2 * QK))]
        return [(raw, lambda hl: SPL[:, slot, hl, :])]

    def ada_after(t, up_only):
        if up_only:
            return 2 if 4 <= t < 8 else 0
        return {4: 2, 5: 1, 6: 1, 7: 1, 8: 1, 9: 1, 10: 1}.get(t, 0)

    def ffn_place(l, t, up_only=False):
        return t + (sum(ada_after(v, up_only) for v in range(t)) if l == 0 else 0)

    def ada_last(up_only):
        t = max(t for t in range(12) if ada_after(t, up_only))
        return ffn_place(0, t, up_only) + ada_after(t, up_only)

    def ffn_ahead(l, t, up_only):
        return ffn_place(l, t + 4, up_only)

    def full_wait(eng, n, rt=0):
        eng.wait_ge(raw_full[n % RAW_SLOTS], 16 * (n // RAW_SLOTS + 1) + 16 * rt)

    @block.sync
    def _(sp):
        sp.dma_start(MATS[:, :], mats).then_inc(consts_in, 16)

        def load(n, src, dst=None, rt=0):
            slot = n % RAW_SLOTS
            if n >= RAW_SLOTS:
                sp.wait_ge(raw_done[slot], n // RAW_SLOTS + rt)
            sp.dma_start(RAW[:, slot, :] if dst is None else dst, src).then_inc(raw_full[slot], 16)

        def tiled(n, k, w):
            return RAW[:, n % RAW_SLOTS, 0:k * w].rearrange("p (k w) -> p k w", k=k)

        def load_chunk(n, l, chunk, rt=0):
            for q in range(ADA_U):
                load_chunk_unit(n + q, l, chunk, q, rt)

        def load_chunk_unit(n, l, chunk, q, rt=0):
            w = ada_w[l].rearrange("(k p) n -> p k n", p=P)
            k = 4 * (q % 4)
            load(n, w[:, k:k + 4, bass.ds(chunk * CHUNK + (q // 4) * 256, 256)], tiled(n, 4, 256), rt)

        for n in range(8):
            src = (ctx if n < 4 else x)[0].rearrange("(t p) d -> t p d", p=P)[(n // 2) % 2]
            load(N_TOK + n, src[:, (n % 2) * UNIT:(n % 2 + 1) * UNIT])
            if n == 1:
                sp.dma_start(ROWS[:, 0, :], norm_g.rearrange("a b (k p) -> (a b k) p", p=P)).then_inc(rows_in, 16)
                for l in range(2):
                    sp.dma_start(ROWS[0:96, 1 + l, :], ada_b[l].rearrange("(k p) -> k p", p=P)).then_inc(rows_in, 16)
                r = 0
                for v in (c[0], c_ctx, pool_scale[0], q_norm[0], kv_norm[0]):
                    k = v.shape[0] // P
                    sp.dma_start(ROWS[r:r + k, 3, :], v.rearrange("(k p) -> k p", p=P)).then_inc(rows_in, 16)
                    r += k
        sp.dma_start(PINV[:, :, :], pool_inv.rearrange("p (g t) -> p g t", g=4)).then_inc(pinv_in, 16)
        with sp.Fori(0, (CHUNKS - LATE) // 2) as i:
            for b in range(2):
                load_chunk(N_ADA0 + b * ADA_U, 0, 2 * i + b, i * (2 * ADA_U // RAW_SLOTS))
        for u in range(8):
            load(N_POOL + u, pool_w[0, u // 2].rearrange("(k p) n -> p k n", p=P)[:, 2 * (u % 2):2 * (u % 2) + 2, :],
                 tiled(N_POOL + u, 2, 512))

        for k in range(LATE):
            load_chunk(N_LATE0 + k * ADA_U, 0, CHUNKS - LATE + k)

        def load_ffn(l, n_base):
            w13 = [w[l].rearrange("(k p) n -> p k n", p=P) for w in (ffn_w1, ffn_w3)]
            w2 = ffn_w2[l].rearrange("(f p) n -> p f n", p=P)
            ada1 = ada_w[1].rearrange("(k p) n -> p k n", p=P)

            def iteration(n, i, rt=0, up_only=False):
                q = 0
                for t in range(2 * W_U + (0 if up_only else W2_U)):
                    k = n + ffn_place(l, t, up_only)
                    if t < 2 * W_U:
                        u = t % W_U
                        load(k, w13[t // W_U][:, 4 * u:4 * u + 4, bass.ds(i * 256, 256)], tiled(k, 4, 256), rt)
                    else:
                        down_unit(k, i - 1, t - 2 * W_U, rt)
                    for v in range(ada_after(t, up_only) if l == 0 else 0):
                        load(k + 1 + v, ada1[:, 2 * q:2 * q + 2, bass.ds(i * CHUNK, CHUNK)], tiled(k + 1 + v, 2, CHUNK), rt)
                        q += 1

            def down_unit(n, i, u, rt=0):
                load(n, w2[:, bass.ds(i * 2, 2), 512 * u:512 * u + 512], tiled(n, 2, 512), rt)

            step = ffn_units(l)
            iteration(n_base, 0, up_only=True)
            n = n_base + step - W2_U
            with sp.Fori(0, (FFN_IT - 2) // 2) as j:
                for b in range(2):
                    iteration(n + b * step, 2 * j + 1 + b, j * (2 * step // RAW_SLOTS))
            n += (FFN_IT - 2) * step
            iteration(n, FFN_IT - 1)
            for u in range(W2_U):
                down_unit(n + step + u, FFN_IT - 1, u)

        load_ffn(0, N_FFN0)
        for k in range(LATE):
            load_chunk(N_LATE1 + k * ADA_U, 1, CHUNKS - LATE + k)
        dqkv = w_dqkv[0].rearrange("(k p) n -> p k n", p=P)
        for u in range(16):
            n = N_DQKV + u
            load(n, dqkv[:, 4 * (u % 4):4 * (u % 4) + 4, 256 * (u // 4):256 * (u // 4) + 256], tiled(n, 4, 256))
        for u in range(2):
            load(N_DQKV + 16 + u, dqkv[:, 8 * u:8 * u + 8, 2 * LORA:2 * LORA + ROPE], tiled(N_DQKV + 16 + u, 8, ROPE))
        sp.wait_ge(norm10["hi"], KT)
        sp.wait_ge(norm10["lo"], KT)
        sp.dma_start(COS, rope_tables[:, 0:SEQ]).then_inc(tables_in, 16)
        sp.dma_start(SIN, rope_tables[:, SEQ:2 * SEQ]).then_inc(tables_in, 16)
        uq = w_uq[0].rearrange("(k p) n -> p k n", p=P)
        ukv = w_ukv[0].rearrange("(k p) n -> p k n", p=P)
        with sp.Fori(0, HEADS // 2) as pair:
            for u in range(2):
                n = N_HEADS + u
                load(n, uq[:, 2 * u:2 * u + 2, bass.ds(pair * (2 * QK), 2 * QK)], tiled(n, 2, 2 * QK), pair)
            for a in range(2):
                n = N_HEADS + 2 + a
                load(n, ukv[:, :, bass.ds(pair * 512 + a * 256, 256)], tiled(n, LT, 256), pair)
        wo = w_o[0].rearrange("(k p) n -> p k n", p=P)
        with sp.Fori(0, 4) as j:
            for b in range(2):
                for u in range(4):
                    n = N_WO + 4 * b + u
                    load(n, wo[:, 4 * u:4 * u + 4, bass.ds(j * 512 + b * 256, 256)], tiled(n, 4, 256), j * 2)
        load_ffn(1, N_FFN1)
        for t in range(2):
            sp.wait_ge(out_a, 2 * (t + 1))
            sp.wait_ge(out_b, 2 * (t + 1))
            sp.dma_start(out[0, t * P:(t + 1) * P, :], OUTT[:, t, :]).then_inc(out_stored, 16)
        sp.wait_ge(out_stored, 32)

    @block.tensor
    def _(pe):
        def mac3(ps, w_hi, w_lo, x_hi, x_lo, first, last):
            nc.tensor.matmul(ps, w_hi, x_hi, start=first, stop=False)
            nc.tensor.matmul(ps, w_hi, x_lo, start=False, stop=False)
            return nc.tensor.matmul(ps, w_lo, x_hi, start=False, stop=last)

        def split_wait(n, rt=0):
            pe.wait_ge(raw_done[n % RAW_SLOTS], n // RAW_SLOTS + 1 + rt)

        def unit(m):
            return SPL[:, m % RAW_SLOTS, 0, :], SPL[:, m % RAW_SLOTS, 1, :]

        def ada_product(n, bank, rt=0):
            for q in range(ADA_U):
                ada_unit(n + q, q, bank, rt)

        def ada_unit(n, q, bank, rt=0):
            full_wait(pe, n, rt)
            c0 = (q // 4) * 256
            for g in range(4):
                mm = nc.tensor.matmul(bank[32 * g:32 * g + 32, c0:c0 + 256], SIL[:, 4 * (q % 4) + g, :],
                                      RAW[:, n % RAW_SLOTS, g * 256:(g + 1) * 256],
                                      start=q % 4 == 0, stop=q % 4 == 3, tile_position=(0, 32 * g))
            mm.then_inc(raw_done[n % RAW_SLOTS], 1)

        def ada_select(row, bank):
            for t in range(4):
                mm = nc.tensor.matmul(bank[:, 2 * t:2 * t + 2], row[:, P * t:P * t + P], SEL, start=True, stop=True)
            mm.then_inc(sel_done, 1)

        def square_sum(s, n_tok):
            pe.wait_ge(s["acc"], s["acc0"] + KT + 2)
            nc.tensor.matmul(PS[7][:, 0:n_tok], ONES[:, :], ACC[:, 0:n_tok], start=True, stop=True).then_inc(s["ss"], 1)

        def square_sums(s, n_tok, beside=None):
            for kt in range(KT):
                if beside is not None:
                    beside(kt)
                pe.wait_ge(s["sq"], s["sq0"] + kt + 1)
                nc.tensor.matmul(PS[7][:, 0:n_tok], ONES[:, :], SQ[:, kt % 2, 0:n_tok], start=kt == 0,
                                 stop=kt == KT - 1).then_inc(s["ss"], 1)

        def late_row(l):
            return CHUNKS - LATE if l == 0 else CHUNKS

        def late_unit(n, l):
            def beside(kt):
                if kt == ADA_U:
                    pe.wait_ge(ada_row, late_row(l) + 1)
                ada_unit(n + kt, kt % ADA_U, PS[4])
            return beside

        def late_selects(l):
            for k in range(LATE):
                chunk = l * CHUNKS + CHUNKS - LATE + k
                pe.wait_ge(ada_row, late_row(l) + k + 1)
                pe.wait_ge(mod_ready, 2 * chunk)
                ada_select(ACC[:, :], PS[5])

        pe.wait_ge(consts_in, 16)
        pe.wait_ge(rows_in, 16 * 8)
        nc.tensor.transpose(PS[4][:, 0:P], ROWS[:, 0, :], IDENT)
        nc.tensor.transpose(PS[4][:, P:P + 96], ROWS[0:96, 1, :], IDENT[0:96, 0:96])
        nc.tensor.transpose(PS[4][:, P + 96:P + 192], ROWS[0:96, 2, :], IDENT[0:96, 0:96])
        nc.tensor.transpose(PS[4][:, S_COL:S_COL + 56], ROWS[0:56, 3, :], IDENT[0:56, 0:56]).then_inc(vec_T, 1)
        for n in range(8):
            full_wait(pe, n)
            if n >= 2:
                pe.wait_ge(tok_a, n - 1)
                pe.wait_ge(tok_b, n - 1)
            for half in range(2):
                for t in range(4):
                    f = (4 * half + t) * P
                    mm = nc.tensor.transpose(PS[2 * (n % 2) + half][:, t * P:(t + 1) * P],
                                             RAW[:, n % RAW_SLOTS, f:f + P], IDENT)
                mm.then_inc(tok_T if half == 0 else raw_done[n % RAW_SLOTS], 1)
        pe.wait_ge(ones_ready, 1)
        square_sum(n0, TOK)

        pe.wait_ge(sil_ready, 2)
        pe.wait_ge(tok_a, 8)
        pe.wait_ge(tok_b, 8)

        def chunk0(n, b, chunk, rt=0, waits=True):
            if waits:
                pe.wait_ge(ada_row, chunk - 1)
            ada_product(n, PS[b], rt)

        def select0(b, chunk, waits=True):
            pe.wait_ge(ada_row, chunk + 1)
            if waits:
                pe.wait_ge(mod_ready, 2 * (chunk - 1))
            ada_select(SQ[:, b, :], PS[2 + b])

        chunk0(N_ADA0, 0, 0, waits=False)
        chunk0(N_ADA0 + ADA_U, 1, 1, waits=False)
        select0(0, 0, waits=False)
        chunk0(N_ADA0 + 2 * ADA_U, 0, 2)
        select0(1, 1, waits=False)
        with pe.Fori(0, (CHUNKS - LATE) // 2 - 2) as j:
            for b in range(2):
                chunk0(N_ADA0 + (3 + b) * ADA_U, (1 + b) % 2, 2 * j + 3 + b, j * (2 * ADA_U // RAW_SLOTS))
                select0(b, 2 * j + 2 + b)
        chunk0(N_ADA0 + (CHUNKS - LATE - 1) * ADA_U, 1, CHUNKS - LATE - 1)
        select0(0, CHUNKS - LATE - 2)
        select0(1, CHUNKS - LATE - 1)

        for u in range(8):
            g, m = u // 2, M_POOL + u
            split_wait(N_POOL + u)
            pe.wait_ge(pool["lo"], 2 * (u + 1))
            w_hi, w_lo = unit(m)
            if u % 2 == 0:
                if g < 2:
                    pe.wait_ge(mod_ready, 2 * (CHUNKS - LATE))
                else:
                    pe.wait_ge(pool["y"], 4 * (g - 1))
            for k2 in range(2):
                kt = 2 * u + k2
                for t in range(4):
                    f = k2 * 512 + t * P
                    mm = mac3(PS[4 * (g % 2) + t][:, :], w_hi[:, f:f + P], w_lo[:, f:f + P],
                              U[:, 0, kt, :], U[:, 1, kt, :], kt % 4 == 0, kt % 4 == 3)
            mm.then_inc(mult_done, 1)

        def run_ffn(l, n_base, m_base, norm, c0, nt):
            s = ffn[l]
            step = ffn_units(l)

            def up(n, m, i, rt=0, first=False):
                if not first:
                    pe.wait_ge(s["silu"], 2 * i)
                for t in range(2 * W_U):
                    mat, u = t // W_U, t % W_U
                    if t == W_U and not first:
                        pe.wait_ge(s["hf"], 2 * i)
                        if l == 0:
                            pe.wait_ge(mod_ready, 2 * (CHUNKS + i))
                    split_wait(n + ffn_place(l, t, first), rt)
                    if first and mat == 0:
                        pe.wait_ge(norm["lo"], 4 * u + 4)
                    w_hi, w_lo = unit(m + t)
                    for k4 in range(4):
                        kt = 4 * u + k4
                        for a in range(2):
                            f = k4 * 256 + a * P
                            mm = mac3(PS[2 * mat + a][:, 0:nt], w_hi[:, f:f + P], w_lo[:, f:f + P],
                                      U[:, 0, kt, c0:c0 + nt], U[:, 1, kt, c0:c0 + nt], kt == 0, kt == KT - 1)
                    mm.then_inc(mult_done, 1)

            def ada_columns(n, i, rt=0):
                pe.wait_ge(raw_done[n % RAW_SLOTS], n // RAW_SLOTS + 1 + rt)
                pe.wait_ge(s["hf"], 2 * (i + 1))
                for t in range(4):
                    for q in range(2):
                        mm = nc.tensor.matmul(PS[3][:, 2 * t + q:2 * t + q + 1], ADA_ACC[:, q, P * t:P * t + P],
                                              ONES[:, 0:1], start=True, stop=True)
                mm.then_inc(sel_done, 1)

            def down_unit(n, m, i, u, slot, rt=0):
                split_wait(n, rt)
                w_hi, w_lo = unit(m)
                for b in range(4):
                    pe.wait_ge(s["y_free"], 16 * i + 4 * u + b + 1)
                    for f2 in range(2):
                        f = f2 * 512 + b * P
                        mm = mac3(PS[4 + b][:, 0:nt], w_hi[:, f:f + P], w_lo[:, f:f + P],
                                  HC[:, slot, 0, f2, 0:nt], HC[:, slot, 1, f2, 0:nt], f2 == 0, f2 == 1)
                    mm.then_inc(s["y"] if b < 3 else mult_done, 1)

            def iteration(n, m, i, slot, rt=0):
                up(n, m, i, rt)
                pe.wait_ge(s["lo"], 2 * i)
                for u in range(W2_U):
                    if l == 0 and u == W2_U - 1:
                        ada_columns(n + ada_last(False), i, rt)
                    down_unit(n + ffn_place(l, 2 * W_U + u), m + 2 * W_U + u, i - 1, u, slot, rt)

            up(n_base, m_base, 0, first=True)
            if l == 0:
                pe.wait_ge(ones_ready, 1)
                ada_columns(n_base + ada_last(True), 0)
            n, m = n_base + step - W2_U, m_base + 8
            with pe.Fori(0, (FFN_IT - 2) // 2) as j:
                for b in range(2):
                    iteration(n + b * step, m + 12 * b, 2 * j + 1 + b, b, j * (2 * step // RAW_SLOTS))
            n, m = n + (FFN_IT - 2) * step, m + (FFN_IT - 2) * 12
            iteration(n, m, FFN_IT - 1, 0)
            pe.wait_ge(s["lo"], 2 * FFN_IT)
            for u in range(W2_U):
                down_unit(n + step + u, m + 12 + u, FFN_IT - 1, u, 1)

        square_sum(norm01, TOK)
        pe.wait_ge(pool["y"], KT)
        square_sums(norm02, TOK, late_unit(N_LATE0, 0))
        late_selects(0)
        run_ffn(0, N_FFN0, M_FFN0, norm02, 0, TOK)

        square_sum(norm03, TOK)
        pe.wait_ge(ffn[0]["y_free"], 4 + 16 * FFN_IT)
        square_sums(norm10, TOK, late_unit(N_LATE1, 1))
        late_selects(1)

        for pr in range(4):
            c0, nt = (CTX, SEQ) if pr < 2 else (0, TOK)
            for u in range(4):
                m = M_DQKV + 4 * pr + u
                split_wait(N_DQKV + 4 * pr + u)
                if pr == 0:
                    pe.wait_ge(norm10["lo"], 4 * u + 4)
                w_hi, w_lo = unit(m)
                for k4 in range(4):
                    kt = 4 * u + k4
                    for a in range(2):
                        f = k4 * 256 + a * P
                        mm = mac3(PS[2 * pr + a][:, 0:nt], w_hi[:, f:f + P], w_lo[:, f:f + P],
                                  U[:, 0, kt, c0:c0 + nt], U[:, 1, kt, c0:c0 + nt], kt == 0, kt == KT - 1)
                mm.then_inc(mult_done, 1)
        pe.wait_ge(dq["evac"], 2)
        for u in range(2):
            split_wait(N_DQKV + 16 + u)
            w_hi, w_lo = unit(M_DQKV + 16 + u)
            for k8 in range(8):
                kt = 8 * u + k8
                mm = mac3(PS[0][:, :], w_hi[:, k8 * P:k8 * P + P], w_lo[:, k8 * P:k8 * P + P],
                          U[:, 0, kt, :], U[:, 1, kt, :], kt == 0, kt == KT - 1)
            mm.then_inc(mult_done, 1)
        pe.wait_ge(dq["sq"], 2)
        for kt in range(LT):
            nc.tensor.matmul(PS[2][:, 0:SEQ], ONES[:, :], LSQ_Q[:, kt, :], start=kt == 0, stop=kt == LT - 1)
        for kt in range(LT):
            mm = nc.tensor.matmul(PS[3][:, :], ONES[:, :], LSQ_KV[:, kt, :], start=kt == 0, stop=kt == LT - 1)
        mm.then_inc(dq["ss"], 1)
        pe.wait_ge(dq["evac"], 9)
        nc.tensor.matmul(PS[4][:, 0:SEQ], SWAP, KRAW[:, CTX:TOK], start=True, stop=True).then_inc(dq["swap"], 1)

        def project(pair, m, rt=0, first=False, vslot=0):
            n = N_HEADS + (m - M_HEADS)
            split_wait(n, rt)
            split_wait(n + 1, rt)
            if first:
                pe.wait_ge(dq["lo"], 8)
                pe.wait_ge(dq["krlo"], 1)
                pe.wait_ge(dq["krhi"], 1)
            else:
                pe.wait_ge(hd["qn_lo"], pair)
                pe.wait_ge(hd["sin"], pair)
                pe.wait_ge(hd["o_lo"], 2 * pair - 2 if not isinstance(pair, int) else max(0, 2 * pair - 2))
            units = [unit(m), unit(m + 1)]

            def cols(k, hl, part):
                w = units[k // 2][hl]
                return w[:, (k % 2) * 2 * QK + part * P:(k % 2) * 2 * QK + (part + 1) * P]

            for part in range(3):
                ps = PS[0][:, part * SEQ:(part + 1) * SEQ] if part < 2 else PS[1][:, 0:SEQ]
                for k in range(LT):
                    mm = mac3(ps, cols(k, 0, part), cols(k, 1, part), QL[:, 0, k, :], QL[:, 1, k, :], k == 0, k == LT - 1)
            mm.then_inc(mult_done, 2)
            for a in range(2):
                split_wait(n + 2 + a, rt)
                w_hi, w_lo = unit(m + 2 + a)
                if not (first and a == 0):
                    pe.wait_ge(hd["kn_lo"], 2 * pair + a)
                for k in range(LT):
                    mm = mac3(PS[2][:, :], w_hi[:, k * 256:k * 256 + P], w_lo[:, k * 256:k * 256 + P],
                              KVL[:, 0, k, :], KVL[:, 1, k, :], k == 0, k == LT - 1)
                mm.then_inc(hd["kpe"], 1)
                if not (first and a == 0):
                    pe.wait_ge(hd["v_lo"], 2 * pair + a)
                for j in range(4):
                    for k in range(LT):
                        f = k * 256 + P
                        mm = mac3(PS[3][:, j * P:(j + 1) * P], KVL[:, 0, k, j * P:(j + 1) * P],
                                  KVL[:, 1, k, j * P:(j + 1) * P], w_hi[:, f:f + P], w_lo[:, f:f + P],
                                  k == 0, k == LT - 1)
                mm.then_inc(mult_done, 1)
                if a == 0:
                    pe.wait_ge(hd["qf"], pair + 1)
                    nc.tensor.matmul(PS[1][:, SEQ:2 * SEQ], SWAP, QF[:, :], start=True, stop=True).then_inc(hd["swap"], 1)

        def scores(pair, a, first=False):
            h = 2 * pair + a
            if first:
                pe.wait_ge(hd["qr_zero"], 2)
            if a == 0:
                pe.wait_ge(hd["qn_lo"], pair + 1)
                pe.wait_ge(hd["qr_lo"], pair + 1)
            pe.wait_ge(hd["kn_lo"], h + 1)
            for qt in range(2):
                if not (first and a == 0):
                    pe.wait_ge(hd["exp"], 2 * h - 1 + qt)
                q = slice(qt * P, (qt + 1) * P)
                mac3(PS[4 + qt][:, :], QN[:, 0, a, q], QN[:, 1, a, q], KN[:, 0, a, :], KN[:, 1, a, :], True, False)
                mac3(PS[4 + qt][:, :], QR[:, 0, a, q], QR[:, 1, a, q], KR[:, 0, :], KR[:, 1, :],
                     False, True).then_inc(hd["s"], 1)

        def turn(pair, a, first=False):
            h = 2 * pair + a
            for qt in range(2):
                pe.wait_ge(hd["p"], 2 * h + qt + 1)
                if not (first and a == 0):
                    pe.wait_ge(hd["pt_lo"], 2 * h - 1 + qt)
                for j in range(4):
                    mm = nc.tensor.transpose(PS[6 + qt][:, j * P:(j + 1) * P], PR[:, a, qt, j * P:(j + 1) * P], IDENT)
                mm.then_inc(hd["pt"], 1)

        def weigh(pair, a, vslot, first=False):
            h = 2 * pair + a
            pe.wait_ge(hd["pt_lo"], 2 * h + 2)
            pe.wait_ge(hd["v_lo"], h + 1)
            pe.wait_ge(hd["sin"], pair + 1)
            if not (first and a == 0):
                pe.wait_ge(hd["o_lo"], h)
            for j in range(4):
                mm = mac3(PS[1][:, a * SEQ:(a + 1) * SEQ], V[:, vslot, 0, a, j * P:(j + 1) * P],
                          V[:, vslot, 1, a, j * P:(j + 1) * P], probs_T(a, 0)[:, j, :], probs_T(a, 1)[:, j, :],
                          j == 0, j == 3)
            mm.then_inc(hd["o"], 1)

        def head_pair(pair, m, vslot, rt=0, first=False):
            project(pair, m, rt)
            turn(pair - 1, 0, first)
            scores(pair, 0)
            turn(pair - 1, 1, first)
            pe.wait_ge(hd["sin"], pair + 1)
            weigh(pair - 1, 0, 1 - vslot, first)
            scores(pair, 1)
            weigh(pair - 1, 1, 1 - vslot, first)

        project(0, M_HEADS, first=True)
        scores(0, 0, first=True)
        scores(0, 1, first=True)
        head_pair(1, M_HEADS + 4, 1, first=True)
        with pe.Fori(0, 3) as j:
            for b in range(2):
                head_pair(2 * j + 2 + b, M_HEADS + 8 + 4 * b, b, j * 2)
        turn(HEADS // 2 - 1, 0)
        turn(HEADS // 2 - 1, 1)
        weigh(HEADS // 2 - 1, 0, 1)
        weigh(HEADS // 2 - 1, 1, 1)

        pe.wait_ge(hd["o_lo"], HEADS)

        def project_out(n, m, dp, bank, rt=0, waits=True):
            for u in range(4):
                split_wait(n + u, rt)
                if u == 0 and waits:
                    pe.wait_ge(wo_y, 2 * dp - 2)
                    pe.wait_ge(norm11["sq"], norm11["sq0"] + 2 * dp - 2)
                w_hi, w_lo = unit(m + u)
                for k4 in range(4):
                    h = 4 * u + k4
                    for a in range(2):
                        f = k4 * 256 + a * P
                        mm = mac3(PS[bank + a][:, 0:SEQ], w_hi[:, f:f + P], w_lo[:, f:f + P],
                                  OT[:, 0, h, :], OT[:, 1, h, :], h == 0, h == HEADS - 1)
                mm.then_inc(mult_done, 1)

        project_out(N_WO, M_WO, 0, 2, waits=False)
        project_out(N_WO + 4, M_WO + 4, 1, 4)
        with pe.Fori(0, 3) as j:
            for b in range(2):
                project_out(N_WO + 8 + 4 * b, M_WO + 8 + 4 * b, 2 * j + 2 + b, 2 + 2 * b, j * 2)

        square_sum(norm11, SEQ)
        square_sums(norm12, SEQ)
        run_ffn(1, N_FFN1, M_FFN1, norm12, CTX, SEQ)
        square_sum(norm13, SEQ)
        for t in range(2):
            for q in range(4):
                pe.wait_ge(norm13["h"], 4 * q + 4)
                if t == 0 and q == 0:
                    pe.wait_ge(norm13["rstd"], norm13["one0"] + 1)
                for j in range(4):
                    kt = 4 * q + j
                    mm = nc.tensor.transpose(PS[4 * t + q][:, j * P:(j + 1) * P],
                                             H[:, kt, CTX + t * P:CTX + (t + 1) * P], IDENT)
                mm.then_inc(out_T, 1)

    @block.scalar
    def _(act):
        def split_hi(n, m, rt=0, mt=0):
            full_wait(act, n, rt)
            if m >= RAW_SLOTS:
                act.wait_ge(mult_done, m - RAW_SLOTS + 1 + mt * RAW_SLOTS)
            for raw, split in unit_parts(n, m):
                ins = nc.scalar.activation(split(0), raw, ACT.Copy)
            ins.then_inc(hi_ready, 1)

        def copy(dst, src):
            return nc.scalar.activation(dst, src, ACT.Copy)

        def square(s, kt, b, src, n_tok, ready=None):
            if ready is not None:
                act.wait_ge(ready[0], ready[1] + kt + 1)
            if s["by_pe"]:
                act.wait_ge(s["ss"], s["ss0"] + kt - 1)
            else:
                act.wait_ge(s["acc"], s["acc0"] + kt + 1)
            nc.scalar.activation(SQ[:, b, 0:n_tok], src(kt), ACT.Square).then_inc(s["sq"], 1)

        def squares(s, src, n_tok, ready=None, first=0, last=KT):
            with act.Fori(0, (last - first) // 2) as j:
                for b in range(2):
                    square(s, 2 * j + first + b, b, src, n_tok, ready)

        def root(s, n_tok):
            act.wait_ge(s["var"], s["one0"] + 1)
            nc.scalar.activation(RSTD[:, 0:n_tok], RSTD[:, 0:n_tok], ACT.Sqrt).then_inc(s["std"], 1)

        def apply_hi(s, l, shift, segs):
            def tile(kt, b):
                act.wait_ge(s["t"], kt + 1)
                for q, c0, w in segs:
                    ins = nc.scalar.activation(U[:, 0, kt, c0:c0 + w], TMP[:, b, c0:c0 + w], ACT.Identity,
                                               bias=MOD[:, l, q, bass.ds(shift * KT + kt, 1)])
                ins.then_inc(s["hi"], 1)
            with act.Fori(0, KT // 2) as j:
                for b in range(2):
                    tile(2 * j + b, b)

        act.wait_ge(vec_T, 1)
        copy(VEC[:, :], PS[4][:, 0:S_COL + 56]).then_inc(vec_ready, 1)
        act.wait_ge(vec_ready, 1)
        act.wait_ge(sil_zero, 1)
        for q in range(2):
            v = VEC[:, S_COL + (1 - q) * KT:S_COL + (2 - q) * KT]
            nc.scalar.activation(SIL[:, :, q], v, ACT.Silu).then_inc(sil_ready, 1)
        for n in range(8):
            act.wait_ge(tok_T, n + 1)
            k = (n % 2) * 8
            copy(H[:, k:k + 4, (n // 2) * P:(n // 2 + 1) * P],
                 PS[2 * (n % 2)][:, :].rearrange("p (k t) -> p k t", k=4)).then_inc(tok_a, 1)
        act.wait_ge(tok_a, 8)
        act.wait_ge(tok_b, 8)
        squares(n0, lambda kt: H[:, kt, :], TOK)
        root(n0, TOK)

        def ada_evac(n, bank, row, rt=0):
            act.wait_ge(raw_done[n % RAW_SLOTS], n // RAW_SLOTS + 1 + rt)
            copy(row, bank[:, :]).then_inc(ada_row, 1)

        act.wait_ge(n0["std"], n0["one0"] + 1)
        for b in range(2):
            ada_evac(N_ADA0 + (b + 1) * ADA_U - 1, PS[b], SQ[:, b, :])

        def evac_pair(j, first_chunk):
            for b in range(2):
                chunk = first_chunk + 2 * j + b
                act.wait_ge(sel_done, chunk - 1)
                ada_evac(N_ADA0 + (first_chunk + b + 1) * ADA_U - 1, PS[b], SQ[:, b, :], j * (2 * ADA_U // RAW_SLOTS))

        with act.Fori(0, 3) as j:
            evac_pair(j, 2)

        def pooled_tile(kt):
            act.wait_ge(pool["t"], kt + 1)
            act.wait_ge(pool["d"], kt + 1)
            for q, c0, w in both:
                ins = nc.scalar.activation(PU[:, q, PAD:PAD + w], TMP[:, 0, c0:c0 + w], ACT.Identity,
                                           bias=MOD[:, 0, q, bass.ds(kt, 1)])
            ins.then_inc(pool["u"], 1)
            act.wait_ge(pool["d"], kt + 2)
            copy(U[:, 0, kt, :], PD[:, :]).then_inc(pool["hi"], 1)

        for b in range(2):
            act.wait_ge(sel_done, 8 + b - 1)
            ada_evac(N_ADA0 + (9 + b) * ADA_U - 1, PS[b], SQ[:, b, :])
            pooled_tile(2 * b)
            pooled_tile(2 * b + 1)
        with act.Fori(0, KT // 2 - 2) as j:
            for b in range(2):
                act.wait_ge(sel_done, 2 * j + 10 + b - 1)
                ada_evac(N_ADA0 + (11 + b) * ADA_U - 1, PS[b], SQ[:, b, :], j * (2 * ADA_U // RAW_SLOTS))
                pooled_tile(2 * j + 4 + b)
        for k in range(4):
            split_hi(N_POOL + k, M_POOL + k)
        for u in range(8):
            if u < 4:
                split_hi(N_POOL + 4 + u, M_POOL + 4 + u)
            if u % 2 == 1:
                act.wait_ge(mult_done, M_POOL + u + 1)
                g = u // 2
                for t in range(4):
                    kt = 4 * g + t
                    nc.scalar.activation(Y[:, kt, :], PS[4 * (g % 2) + t][:, :], ACT.Copy,
                                         scale=VEC[:, PS_COL + kt:PS_COL + kt + 1]).then_inc(pool["y"], 1)
                squares(norm01, lambda kt: Y[:, kt, :], TOK, (pool["y"], 0), 4 * g, 4 * g + 4)

        def prime(n, m):
            for k in range(RAW_SLOTS):
                split_hi(n + k, m + k)

        def run_ffn(l, n_base, m_base, nt, after):
            s = ffn[l]
            step = ffn_units(l)

            def iteration(n, m, i, slot, rt=0, mt=0, up_only=False):
                for t in range(W_U):
                    split_hi(n + ffn_ahead(l, t, up_only), m + t + 4, rt, mt)
                act.wait_ge(s["lo"], 2 * i)
                act.wait_ge(mult_done, m + W_U + mt * RAW_SLOTS)
                for a in range(2):
                    nc.scalar.activation(SQ[:, a, 0:nt], PS[a][:, 0:nt], ACT.Silu).then_inc(s["silu"], 1)
                for t in range(W_U, 2 * W_U):
                    split_hi(n + ffn_ahead(l, t, up_only), m + t + 4, rt, mt)
                for a in range(2):
                    act.wait_ge(s["hf"], 2 * i + a + 1)
                    copy(HC[:, slot, 0, a, 0:nt], SQ[:, a, 0:nt]).then_inc(s["hi"], 1)
                for t in range(2 * W_U, 2 * W_U + (0 if up_only else W2_U)):
                    split_hi(n + ffn_ahead(l, t, up_only), m + t + 4, rt, mt)

            iteration(n_base, m_base, 0, 0, up_only=True)
            n, m = n_base + step - W2_U, m_base + 8
            with act.Fori(0, (FFN_IT - 2) // 2) as j:
                for b in range(2):
                    iteration(n + b * step, m + 12 * b, 2 * j + 1 + b, 1 - b, j * (2 * step // RAW_SLOTS), j * 6)
            iteration(n + (FFN_IT - 2) * step, m + (FFN_IT - 2) * 12, FFN_IT - 1, 1)
            act.wait_ge(s["lo"], 2 * FFN_IT)
            squares(after, lambda kt: Y[:, kt, 0:nt], nt, (s["y_free"], 4 + 16 * (FFN_IT - 1)))

        def late_evac(l, n, k):
            act.wait_ge(mod_ready, 2 * (l * CHUNKS + CHUNKS - LATE + k))
            ada_evac(n + (k + 1) * ADA_U - 1, PS[4], ACC[:, :])

        def late_stage(s, l, n, n_next, m_next):
            squares(s, lambda kt: H[:, kt, :], TOK, (s["after"], 0), 0, 8)
            late_evac(l, n, 0)
            squares(s, lambda kt: H[:, kt, :], TOK, (s["after"], 0), 8, 16)
            prime(n_next, m_next)
            root(s, TOK)
            late_evac(l, n, 1)

        root(norm01, TOK)
        late_stage(norm02, 0, N_LATE0, N_FFN0, M_FFN0)
        apply_hi(norm02, 0, 3, both)
        run_ffn(0, N_FFN0, M_FFN0, TOK, norm03)
        root(norm03, TOK)
        late_stage(norm10, 1, N_LATE1, N_DQKV, M_DQKV)
        apply_hi(norm10, 1, 0, both)

        for pr in range(4):
            for u in range(4):
                k = 4 * pr + u + 4
                if k < DQKV_U:
                    split_hi(N_DQKV + k, M_DQKV + k)
            act.wait_ge(mult_done, M_DQKV + 4 * pr + 4)
            for a in range(2):
                dst = CQ[:, 2 * pr + a, :] if pr < 2 else CKV[:, 2 * pr - 4 + a, :]
                nt = SEQ if pr < 2 else TOK
                copy(dst, PS[2 * pr + a][:, 0:nt]).then_inc(dq["evac"], 1)
        act.wait_ge(dq["evac"], 8)
        nc.scalar.activation(LSQ_Q[:, :, :], CQ[:, :, :], ACT.Square).then_inc(dq["sq"], 1)
        nc.scalar.activation(LSQ_KV[:, :, :], CKV[:, :, :], ACT.Square).then_inc(dq["sq"], 1)
        act.wait_ge(mult_done, M_DQKV + DQKV_U)
        copy(KRAW[:, :], PS[0][:, :]).then_inc(dq["evac"], 1)
        act.wait_ge(dq["var"], 2)
        nc.scalar.activation(RSTDQ[:, :], RSTDQ[:, :], ACT.Sqrt).then_inc(dq["std"], 1)
        nc.scalar.activation(RSTD[:, :], RSTD[:, :], ACT.Sqrt).then_inc(dq["std"], 1)
        for k in range(LT):
            act.wait_ge(dq["t"], k + 1)
            copy(QL[:, 0, k, :], CQ[:, k, :]).then_inc(dq["hi"], 1)
        for k in range(LT):
            act.wait_ge(dq["t"], LT + k + 1)
            copy(KVL[:, 0, k, :], CKV[:, k, :]).then_inc(dq["hi"], 1)
        act.wait_ge(dq["rot"], 1)
        copy(KR[:, 0, 0:CTX], KRAW[:, 0:CTX])
        copy(KR[:, 0, CTX:TOK], KROT[:, :]).then_inc(dq["krhi"], 1)
        for u in range(4):
            split_hi(N_HEADS + u, M_HEADS + u)

        def next_unit(pair, u, rt, mt, m, last):
            if not last:
                k = 4 + u + (m - M_HEADS)
                split_hi(N_HEADS + k, M_HEADS + k, rt, mt)

        def head_project(pair, m, vslot, rt=0, mt=0, last=False):
            act.wait_ge(mult_done, m + 2 + mt * RAW_SLOTS)
            if not (isinstance(pair, int) and pair == 0):
                act.wait_ge(hd["s"], 4 * pair)
                act.wait_ge(hd["qr_lo"], pair)
            copy(QN[:, 0, :, :], PS[0][:, :].rearrange("p (h q) -> p h q", h=2)).then_inc(hd["qn_hi"], 1)
            copy(QF[:, :], PS[1][:, 0:SEQ]).then_inc(hd["qf"], 1)
            next_unit(pair, 0, rt, mt, m, last)
            next_unit(pair, 1, rt, mt, m, last)
            for a in range(2):
                act.wait_ge(hd["kpe"], 2 * pair + a + 1)
                copy(KN[:, 0, a, :], PS[2][:, :]).then_inc(hd["kn_hi"], 1)
                act.wait_ge(mult_done, m + 3 + a + mt * RAW_SLOTS)
                copy(V[:, vslot, 0, a, :], PS[3][:, :]).then_inc(hd["v_hi"], 1)
                next_unit(pair, 2 + a, rt, mt, m, last)
                if a == 0:
                    act.wait_ge(hd["rot"], pair + 1)
                    copy(QR[0:ROPE, 0, 0, :], QF[0:ROPE, :])
                    copy(QR[ROPE:P, 0, 1, :], QF[ROPE:P, :]).then_inc(hd["qr_hi"], 1)

        def exps(pair, a):
            for qt in range(2):
                k = 4 * pair + 2 * a + qt
                act.wait_ge(hd["nmax"], k + 1)
                if not (isinstance(pair, int) and pair == 0):
                    act.wait_ge(hd["pt"], k - 3)
                nc.scalar.activation(PR[:, a, qt, :], PS[4 + qt][:, :], ACT.Exp, bias=SMALL[:, 1, 2 * a + qt:2 * a + qt + 1],
                                     scale=SCALE, accum_out=SMALL[:, 2, 2 * a + qt:2 * a + qt + 1]).then_inc(hd["exp"], 1)

        def weigh_hi(pair, a):
            h = 2 * pair + a
            for qt in range(2):
                act.wait_ge(hd["pt"], 2 * h + qt + 1)
                if not (isinstance(pair, int) and pair == 0):
                    act.wait_ge(hd["o"], h - 1)
                copy(probs_T(a, 0)[:, :, qt * P:(qt + 1) * P],
                     PS[6 + qt][:, :].rearrange("p (j q) -> p j q", j=4)).then_inc(hd["pt_hi"], 1)

        def out_hi(pair, a):
            h = 2 * pair + a
            act.wait_ge(hd["o"], h + 1)
            dst = OT[:, 0, h, :] if isinstance(h, int) else OT[:, 0, bass.ds(h, 1), :].rearrange("p a q -> p (a q)")
            copy(dst, PS[1][:, a * SEQ:(a + 1) * SEQ]).then_inc(hd["o_hi"], 1)

        def head_pair(pair, m, vslot, rt=0, mt=0, last=False):
            head_project(pair, m, vslot, rt, mt, last)
            weigh_hi(pair - 1, 0)
            exps(pair, 0)
            weigh_hi(pair - 1, 1)
            out_hi(pair - 1, 0)
            exps(pair, 1)
            out_hi(pair - 1, 1)

        head_project(0, M_HEADS, 0)
        exps(0, 0)
        exps(0, 1)
        head_pair(1, M_HEADS + 4, 1)
        with act.Fori(0, 2) as j:
            for b in range(2):
                head_pair(2 * j + 2 + b, M_HEADS + 8 + 4 * b, b, j * 2, j * 2)
        head_pair(6, M_HEADS + 24, 0)
        head_pair(7, M_HEADS + 28, 1, last=True)
        for u in range(4):
            split_hi(N_WO + u, M_WO + u)
        for a in range(2):
            weigh_hi(HEADS // 2 - 1, a)
        for a in range(2):
            out_hi(HEADS // 2 - 1, a)

        def out_evac(dp, m, bank, mt=0):
            act.wait_ge(mult_done, m + 4 + mt * RAW_SLOTS)
            for a in range(2):
                square(norm11, 2 * dp + a, a, lambda kt: PS[bank + a][:, 0:SEQ], SEQ)
            for a in range(2):
                copy(Y1[:, 2 * dp + a, :], PS[bank + a][:, 0:SEQ]).then_inc(wo_y, 1)

        act.wait_ge(hd["pt_lo"], 2 * HEADS)
        with act.Fori(0, 3) as j:
            for b in range(2):
                for u in range(4):
                    split_hi(N_WO + 4 + 4 * b + u, M_WO + 4 + 4 * b + u, j * 2, j * 2)
                out_evac(2 * j + b, M_WO + 4 * b, 2 + 2 * b, j * 2)
        for u in range(4):
            split_hi(N_WO + 28 + u, M_WO + 28 + u)
        out_evac(6, M_WO + 24, 2)
        out_evac(7, M_WO + 28, 4)

        prime(N_FFN1, M_FFN1)
        root(norm11, SEQ)
        squares(norm12, lambda kt: H[:, kt, CTX:TOK], SEQ, (norm11["h"], 0))
        root(norm12, SEQ)
        apply_hi(norm12, 1, 3, latent)
        run_ffn(1, N_FFN1, M_FFN1, SEQ, norm13)
        root(norm13, SEQ)
        for t in range(2):
            for q in (0, 2):
                act.wait_ge(out_T, 4 * t + q + 1)
                copy(OUTT[:, t, 512 * q:512 * q + 512], PS[4 * t + q][:, :]).then_inc(out_a, 1)

    @block.vector
    def _(dve):
        def split_lo(n, m, rt=0, mt=0):
            dve.wait_ge(hi_ready, m + 1 + mt * RAW_SLOTS)
            for raw, split in unit_parts(n, m):
                ins = nc.vector.tensor_tensor(split(1), raw, split(0).bitcast(F32), ALU.subtract)
            ins.then_inc(raw_done[n % RAW_SLOTS], 1)

        def low(dst, src, hi):
            return nc.vector.tensor_tensor(dst, src, hi.bitcast(F32), ALU.subtract)

        def clear_sum(s, n_tok):
            nc.vector.memset(ACC[:, 0:n_tok], 0.0).then_inc(s["acc"], 2)

        def add_square(s, kt, b, n_tok):
            dve.wait_ge(s["sq"], s["sq0"] + kt + 1)
            dve.wait_ge(s["acc"], s["acc0"] + kt + 2)
            nc.vector.tensor_tensor(ACC[:, 0:n_tok], ACC[:, 0:n_tok], SQ[:, b, 0:n_tok], ALU.add).then_inc(s["acc"], 1)

        def add_squares(s, n_tok, first=0, last=KT):
            with dve.Fori(0, (last - first) // 2) as j:
                for b in range(2):
                    add_square(s, 2 * j + first + b, b, n_tok)

        def reciprocal_root(s, n_tok):
            dve.wait_ge(s["ss"], s["ss0"] + s["ss1"])
            nc.vector.tensor_scalar(RSTD[:, 0:n_tok], PS[7][:, 0:n_tok], 1.0 / D, EPS, ALU.mult, ALU.add).then_inc(s["var"], 1)
            dve.wait_ge(s["std"], s["one0"] + 1)
            nc.vector.reciprocal(RSTD[:, 0:n_tok], RSTD[:, 0:n_tok]).then_inc(s["rstd"], 1)
            dve.wait_ge(s["rstd"], s["one0"] + 1)

        def update(s, src, col, segs, c0, n_tok):
            def product(kt, b, waits=True):
                if waits:
                    dve.wait_ge(s["h"], kt - 1)
                for q, t0, w in segs:
                    o = t0 - c0
                    ins = nc.vector.scalar_tensor_tensor(TMP[:, b, o:o + w], src(kt, o, w), COL[:, col, q, bass.ds(kt, 1)],
                                                         RSTD[:, o:o + w], ALU.mult, ALU.mult)
                ins.then_inc(s["t"], 1)

            def add(kt, b):
                dve.wait_ge(s["t"], kt + 1)
                nc.vector.tensor_tensor(H[:, kt, c0:c0 + n_tok], H[:, kt, c0:c0 + n_tok], TMP[:, b, 0:n_tok],
                                        ALU.add).then_inc(s["h"], 1)

            product(0, 0, waits=False)
            product(1, 1, waits=False)
            add(0, 0)
            with dve.Fori(0, KT // 2 - 1) as j:
                for b in range(2):
                    product(2 * j + 2 + b, b)
                    add(2 * j + 1 + b, 1 - b)
            add(KT - 1, 1)

        def apply(s, l, shift, col, segs, c0):
            def product(kt, b, waits=True):
                if waits:
                    dve.wait_ge(s["lo"], kt - 1)
                for q, t0, w in segs:
                    ins = nc.vector.scalar_tensor_tensor(TMP[:, b, t0:t0 + w], H[:, kt, t0:t0 + w],
                                                         COL[:, col, q, bass.ds(kt, 1)],
                                                         RSTD[:, t0 - c0:t0 - c0 + w], ALU.mult, ALU.mult)
                ins.then_inc(s["t"], 1)

            def lo(kt, b):
                dve.wait_ge(s["hi"], kt + 1)
                for q, t0, w in segs:
                    ins = nc.vector.scalar_tensor_tensor(U[:, 1, kt, t0:t0 + w], TMP[:, b, t0:t0 + w],
                                                         MOD[:, l, q, bass.ds(shift * KT + kt, 1)],
                                                         U[:, 0, kt, t0:t0 + w].bitcast(F32), ALU.add, ALU.subtract)
                ins.then_inc(s["lo"], 1)

            product(0, 0, waits=False)
            product(1, 1, waits=False)
            lo(0, 0)
            with dve.Fori(0, KT // 2 - 1) as j:
                for b in range(2):
                    product(2 * j + 2 + b, b)
                    lo(2 * j + 1 + b, 1 - b)
            lo(KT - 1, 1)

        def mod_columns(l, chunk, ct, bank):
            dve.wait_ge(sel_done, chunk + 1)
            for q in range(2):
                nc.vector.tensor_tensor(MOD[:, l, q, bass.ds(ct * 4, 4)], bank[:, q:8:2],
                                        VEC[:, bass.ds(B_COL + 96 * l + ct * 4, 4)], ALU.add).then_inc(mod_ready, 1)

        def scale_gate(l, part):
            for q in range(2):
                j = (1, 2, 4, 5)[part]
                src = MOD[:, l, q, j * KT:(j + 1) * KT]
                g = VEC[:, G_COL + (4 * l + part) * KT:G_COL + (4 * l + part + 1) * KT]
                if part % 2 == 0:
                    ins = nc.vector.scalar_tensor_tensor(COL[:, 4 * l + part, q, :], src, 1.0, g, ALU.add, ALU.mult)
                else:
                    ins = nc.vector.tensor_tensor(COL[:, 4 * l + part, q, :], src, g, ALU.mult)
            ins.then_inc(col_ready, 1)
            dve.wait_ge(col_ready, 4 * l + part + 1)

        for n in range(8):
            dve.wait_ge(raw_done[n % RAW_SLOTS], n // RAW_SLOTS + 1)
            k = (n % 2) * 8 + 4
            nc.vector.tensor_copy(H[:, k:k + 4, (n // 2) * P:(n // 2 + 1) * P],
                                  PS[2 * (n % 2) + 1][:, :].rearrange("p (k t) -> p k t", k=4)).then_inc(tok_b, 1)
        clear_sum(n0, TOK)
        add_squares(n0, TOK)
        reciprocal_root(n0, TOK)
        dve.wait_ge(vec_ready, 1)
        with dve.Fori(0, 4) as j:
            for b in range(2):
                mod_columns(0, 2 * j + b, 2 * j + b, PS[2 + b])
        dve.wait_ge(mod_ready, 16)
        scale_gate(0, 0)
        dve.wait_ge(pinv_in, 16)

        def pooled_tile(kt, g):
            for q, t0, w in both:
                ins = nc.vector.scalar_tensor_tensor(TMP[:, 0, t0:t0 + w], H[:, kt, t0:t0 + w],
                                                     COL[:, 0, q, bass.ds(kt, 1)], RSTD[:, t0:t0 + w],
                                                     ALU.mult, ALU.mult)
            ins.then_inc(pool["t"], 1)
            dve.wait_ge(pool["s"], kt + 1)
            total = (PA, PB, PA, PB)[g]
            for q in range(2):
                ins = nc.vector.tensor_tensor(PD[:, q * SEQ:(q + 1) * SEQ], total[:, q, PAD:PAD + SEQ],
                                              PINV[:, g, :], ALU.mult)
            ins.then_inc(pool["m"], 1)
            dve.wait_ge(pool["m"], kt + 1)
            by_seq = PD[:, :].rearrange("p (q t) -> p q t", q=2)
            nc.vector.tensor_tensor(by_seq, by_seq, PU[:, :, PAD:PAD + SEQ], ALU.subtract).then_inc(pool["d"], 1)
            dve.wait_ge(pool["d"], kt + 2)
            dve.wait_ge(pool["hi"], kt + 1)
            low(U[:, 1, kt, :], PD[:, :], U[:, 0, kt, :]).then_inc(pool["lo"], 1)

        for b in range(2):
            for kt in (2 * b, 2 * b + 1):
                pooled_tile(kt, 0)
                dve.wait_ge(pool["lo"], kt + 1)
            mod_columns(0, 8 + b, 8 + b, PS[2 + b])
        for g in range(1, 4):
            with dve.Fori(0, 2) as j:
                for b in range(2):
                    kt = 2 * j + 4 * g + b
                    pooled_tile(kt, g)
                    mod_columns(0, 6 + kt, 6 + kt, PS[2 + b])
                    dve.wait_ge(pool["lo"], kt + 1)

        def prime(n, m):
            for k in range(RAW_SLOTS):
                split_lo(n + k, m + k)

        prime(N_POOL, M_POOL)
        dve.wait_ge(mod_ready, 2 * (CHUNKS - LATE))
        scale_gate(0, 1)
        scale_gate(0, 2)
        clear_sum(norm01, TOK)
        for g in range(4):
            if g < 2:
                for k in range(2 * g, 2 * g + 2):
                    split_lo(N_POOL + 4 + k, M_POOL + 4 + k)
            add_squares(norm01, TOK, 4 * g, 4 * g + 4)

        def run_ffn(l, n_base, m_base, nt, after):
            s = ffn[l]
            step = ffn_units(l)

            def hidden(m, i, mt):
                for a in range(2):
                    dve.wait_ge(s["silu"], 2 * i + a + 1)
                    dve.wait_ge(mult_done, m + 2 * W_U + mt * RAW_SLOTS)
                    nc.vector.tensor_tensor(SQ[:, a, 0:nt], SQ[:, a, 0:nt], PS[2 + a][:, 0:nt],
                                            ALU.mult).then_inc(s["hf"], 1)

            def hidden_lo(i, slot):
                for a in range(2):
                    dve.wait_ge(s["hf"], 2 * i + a + 1)
                    dve.wait_ge(s["hi"], 2 * i + a + 1)
                    low(HC[:, slot, 1, a, 0:nt], SQ[:, a, 0:nt], HC[:, slot, 0, a, 0:nt]).then_inc(s["lo"], 1)

            def ada_unit(n, q, i, before, rt):
                full_wait(dve, n, rt)
                if q == 0:
                    dve.wait_ge(sel_done, CHUNKS + i)
                else:
                    dve.wait_ge(raw_done[before % RAW_SLOTS], before // RAW_SLOTS + 1 + rt)
                for k in range(2):
                    for g in range(2):
                        dst, w = ADA_ACC[:, g, :], RAW[:, n % RAW_SLOTS, k * CHUNK:(k + 1) * CHUNK]
                        silu_c = SIL[:, 2 * q + k, g:g + 1]
                        if k == 1:
                            dve.wait_ge(ada_acc, 2 * (ADA_U * i + q) + g + 1)
                        if q == 0 and k == 0:
                            ins = nc.vector.tensor_scalar(dst, w, silu_c, 0.0, ALU.mult, ALU.add)
                        else:
                            ins = nc.vector.scalar_tensor_tensor(dst, w, silu_c, dst, ALU.mult, ALU.add)
                        if k == 0:
                            ins.then_inc(ada_acc, 1)
                ins.then_inc(raw_done[n % RAW_SLOTS], 1)

            def split_ahead(n, m, i, t, up_only=False, rt=0, mt=0):
                split_lo(n + ffn_ahead(l, t, up_only), m + t + 4, rt, mt)
                if l == 0:
                    q = sum(ada_after(v, up_only) for v in range(t + 4))
                    places = [ffn_place(0, v, up_only) + 1 + k for v in range(12) for k in range(ada_after(v, up_only))]
                    for k in range(ada_after(t + 4, up_only)):
                        ada_unit(n + places[q + k], q + k, i, n + places[q + k - 1], rt)

            def add_down(m, i, u, mt=0):
                for b in range(4):
                    if b < 3:
                        dve.wait_ge(s["y"], 3 * (4 * i + u) + b + 1)
                    else:
                        dve.wait_ge(mult_done, m + 1 + mt * RAW_SLOTS)
                    kt = 4 * u + b
                    nc.vector.tensor_tensor(Y[:, kt, 0:nt], Y[:, kt, 0:nt], PS[4 + b][:, 0:nt],
                                            ALU.add).then_inc(s["y_free"], 1)

            def iteration(n, m, i, slot, rt=0, mt=0):
                for t in range(2 * W_U - 1):
                    split_ahead(n, m, i, t, False, rt, mt)
                hidden(m, i, mt)
                dve.wait_ge(s["y_free"], 4 + 16 * (i - 1))
                for u in range(W2_U):
                    add_down(m + 2 * W_U + u, i - 1, u, mt)
                    if u == 0:
                        split_ahead(n, m, i, 2 * W_U - 1, False, rt, mt)
                    split_ahead(n, m, i, 2 * W_U + u, False, rt, mt)
                hidden_lo(i, slot)
                if l == 0:
                    mod_columns(1, CHUNKS + i, i, PS[3])

            if l == 0:
                dve.wait_ge(sil_ready, 2)
                dve.wait_ge(norm02["lo"], KT)
            for t in range(2 * W_U - 1):
                split_ahead(n_base, m_base, 0, t, True)
            hidden(m_base, 0, 0)
            hidden_lo(0, 0)
            split_ahead(n_base, m_base, 0, 2 * W_U - 1, True)
            if l == 0:
                mod_columns(1, CHUNKS, 0, PS[3])
            n, m = n_base + step - W2_U, m_base + 8
            with dve.Fori(0, (FFN_IT - 2) // 2) as j:
                for b in range(2):
                    iteration(n + b * step, m + 12 * b, 2 * j + 1 + b, 1 - b, j * (2 * step // RAW_SLOTS), j * 6)
            n, m = n + (FFN_IT - 2) * step, m + (FFN_IT - 2) * 12
            iteration(n, m, FFN_IT - 1, 1)
            dve.wait_ge(s["y_free"], 4 + 16 * (FFN_IT - 1))
            clear_sum(after, nt)
            for u in range(W2_U):
                add_down(m + 12 + u, FFN_IT - 1, u)
                if u:
                    add_squares(after, nt, 4 * u - 4, 4 * u)
            add_squares(after, nt, KT - 4, KT)

        reciprocal_root(norm01, TOK)
        update(norm01, lambda kt, o, w: Y[:, kt, o:o + w], 1, both, 0, TOK)
        prime(N_FFN0, M_FFN0)
        reciprocal_root(norm02, TOK)
        mod_columns(0, CHUNKS - 2, CHUNKS - 2, PS[5])
        apply(norm02, 0, 3, 2, both, 0)
        mod_columns(0, CHUNKS - 1, CHUNKS - 1, PS[5])
        dve.wait_ge(mod_ready, 2 * CHUNKS)
        scale_gate(0, 3)
        run_ffn(0, N_FFN0, M_FFN0, TOK, norm03)
        reciprocal_root(norm03, TOK)
        update(norm03, lambda kt, o, w: Y[:, kt, o:o + w], 3, both, 0, TOK)
        prime(N_DQKV, M_DQKV)
        for part in range(3):
            scale_gate(1, part)
        reciprocal_root(norm10, TOK)
        mod_columns(1, 2 * CHUNKS - 2, CHUNKS - 2, PS[5])
        apply(norm10, 1, 0, 4, both, 0)
        mod_columns(1, 2 * CHUNKS - 1, CHUNKS - 1, PS[5])
        dve.wait_ge(mod_ready, 4 * CHUNKS)
        scale_gate(1, 3)

        for k in range(4, DQKV_U):
            split_lo(N_DQKV + k, M_DQKV + k)
        dve.wait_ge(dq["ss"], 1)
        nc.vector.tensor_scalar(RSTDQ[:, :], PS[2][:, 0:SEQ], 1.0 / LORA, EPS, ALU.mult, ALU.add).then_inc(dq["var"], 1)
        nc.vector.tensor_scalar(RSTD[:, :], PS[3][:, :], 1.0 / LORA, EPS, ALU.mult, ALU.add).then_inc(dq["var"], 1)
        dve.wait_ge(dq["std"], 2)
        nc.vector.reciprocal(RSTDQ[:, :], RSTDQ[:, :]).then_inc(dq["rstd"], 1)
        nc.vector.reciprocal(RSTD[:, :], RSTD[:, :]).then_inc(dq["rstd"], 1)
        dve.wait_ge(dq["rstd"], 2)
        for k in range(2 * LT):
            kind, i = divmod(k, LT)
            lat, r, g = ((CQ, RSTDQ, QN_COL), (CKV, RSTD, KVN_COL))[kind]
            nc.vector.scalar_tensor_tensor(lat[:, i, :], lat[:, i, :], VEC[:, g + i:g + i + 1], r[:, :],
                                           ALU.mult, ALU.mult).then_inc(dq["t"], 1)
        for k in range(2 * LT):
            kind, i = divmod(k, LT)
            lat, dst = ((CQ, QL), (CKV, KVL))[kind]
            dve.wait_ge(dq["t"], k + 1)
            dve.wait_ge(dq["hi"], k + 1)
            low(dst[:, 1, i, :], lat[:, i, :], dst[:, 0, i, :]).then_inc(dq["lo"], 1)
        dve.wait_ge(tables_in, 32)
        dve.wait_ge(dq["swap"], 1)
        nc.vector.tensor_tensor(KSIN[:, :], SIN, PS[4][:, 0:SEQ], ALU.mult).then_inc(dq["sin"], 1)
        nc.vector.tensor_tensor(KROT[:, :], COS, KRAW[:, CTX:TOK], ALU.mult).then_inc(dq["cos"], 1)
        dve.wait_ge(dq["sin"], 1)
        dve.wait_ge(dq["cos"], 1)
        nc.vector.tensor_tensor(KROT[:, :], KROT[:, :], KSIN[:, :], ALU.add).then_inc(dq["rot"], 1)
        dve.wait_ge(dq["rot"], 1)
        dve.wait_ge(dq["krhi"], 1)
        low(KR[:, 1, 0:CTX], KRAW[:, 0:CTX], KR[:, 0, 0:CTX])
        low(KR[:, 1, CTX:TOK], KROT[:, :], KR[:, 0, CTX:TOK]).then_inc(dq["krlo"], 1)
        for u in range(4):
            split_lo(N_HEADS + u, M_HEADS + u)

        def next_unit(u, rt, mt, m, last):
            if not last:
                k = 4 + u + (m - M_HEADS)
                split_lo(N_HEADS + k, M_HEADS + k, rt, mt)

        def head_project(pair, m, vslot, rt=0, mt=0, last=False):
            dve.wait_ge(hd["qn_hi"], pair + 1)
            low(QN[:, 1, :, :], PS[0][:, :].rearrange("p (h q) -> p h q", h=2), QN[:, 0, :, :]).then_inc(hd["qn_lo"], 1)
            next_unit(0, rt, mt, m, last)
            next_unit(1, rt, mt, m, last)
            for a in range(2):
                dve.wait_ge(hd["kn_hi"], 2 * pair + a + 1)
                low(KN[:, 1, a, :], PS[2][:, :], KN[:, 0, a, :]).then_inc(hd["kn_lo"], 1)
                dve.wait_ge(hd["v_hi"], 2 * pair + a + 1)
                low(V[:, vslot, 1, a, :], PS[3][:, :], V[:, vslot, 0, a, :]).then_inc(hd["v_lo"], 1)
                if a == 0:
                    dve.wait_ge(hd["swap"], pair + 1)
                    nc.vector.tensor_tensor(QS[:, :], SIN, PS[1][:, SEQ:2 * SEQ], ALU.mult).then_inc(hd["sin"], 1)
                    nc.vector.tensor_tensor(QF[:, :], COS, QF[:, :], ALU.mult).then_inc(hd["cos"], 1)
                    dve.wait_ge(hd["sin"], pair + 1)
                    dve.wait_ge(hd["cos"], pair + 1)
                    nc.vector.tensor_tensor(QF[:, :], QF[:, :], QS[:, :], ALU.add).then_inc(hd["rot"], 1)
                next_unit(2 + a, rt, mt, m, last)
                if a == 1:
                    dve.wait_ge(hd["rot"], pair + 1)
                    dve.wait_ge(hd["qr_hi"], pair + 1)
                    low(QR[0:ROPE, 1, 0, :], QF[0:ROPE, :], QR[0:ROPE, 0, 0, :])
                    low(QR[ROPE:P, 1, 1, :], QF[ROPE:P, :], QR[ROPE:P, 0, 1, :]).then_inc(hd["qr_lo"], 1)

        def maxima(pair, a):
            for qt in range(2):
                k, col = 4 * pair + 2 * a + qt, 2 * a + qt
                dve.wait_ge(hd["s"], k + 1)
                nc.vector.reduce_max(SMALL[:, 0, col:col + 1], PS[4 + qt][:, :], AX.X).then_inc(hd["max"], 1)
                dve.wait_ge(hd["max"], k + 1)
                nc.vector.tensor_scalar(SMALL[:, 1, col:col + 1], SMALL[:, 0, col:col + 1], -SCALE, None,
                                        ALU.mult).then_inc(hd["nmax"], 1)

        def normalise(pair, a):
            for qt in range(2):
                k, col = 4 * pair + 2 * a + qt, 2 * a + qt
                dve.wait_ge(hd["exp"], k + 1)
                nc.vector.reciprocal(SMALL[:, 3, col:col + 1], SMALL[:, 2, col:col + 1]).then_inc(hd["rinv"], 1)
                dve.wait_ge(hd["rinv"], k + 1)
                nc.vector.tensor_scalar(PR[:, a, qt, :], PR[:, a, qt, :], SMALL[:, 3, col:col + 1], None,
                                        ALU.mult).then_inc(hd["p"], 1)

        def weigh_lo(pair, a):
            h = 2 * pair + a
            for qt in range(2):
                dve.wait_ge(hd["pt_hi"], 2 * h + qt + 1)
                q = slice(qt * P, (qt + 1) * P)
                low(probs_T(a, 1)[:, :, q], PS[6 + qt][:, :].rearrange("p (j q) -> p j q", j=4),
                    probs_T(a, 0)[:, :, q]).then_inc(hd["pt_lo"], 1)

        def out_lo(pair, a):
            h = 2 * pair + a
            dve.wait_ge(hd["o_hi"], h + 1)
            low(OT[:, 1, h, :], PS[1][:, a * SEQ:(a + 1) * SEQ], OT[:, 0, h, :]).then_inc(hd["o_lo"], 1)

        def head_pair(pair, m, vslot, rt=0, mt=0, last=False):
            head_project(pair, m, vslot, rt, mt, last)
            weigh_lo(pair - 1, 0)
            maxima(pair, 0)
            weigh_lo(pair - 1, 1)
            normalise(pair, 0)
            out_lo(pair - 1, 0)
            maxima(pair, 1)
            out_lo(pair - 1, 1)
            normalise(pair, 1)

        head_project(0, M_HEADS, 0)
        for a in range(2):
            maxima(0, a)
            normalise(0, a)
        head_pair(1, M_HEADS + 4, 1)
        with dve.Fori(0, 2) as j:
            for b in range(2):
                head_pair(2 * j + 2 + b, M_HEADS + 8 + 4 * b, b, j * 2, j * 2)
        head_pair(6, M_HEADS + 24, 0)
        head_pair(7, M_HEADS + 28, 1, last=True)
        prime(N_WO, M_WO)
        for a in range(2):
            weigh_lo(HEADS // 2 - 1, a)
        for a in range(2):
            out_lo(HEADS // 2 - 1, a)
        clear_sum(norm11, SEQ)
        with dve.Fori(0, 3) as j:
            for b in range(2):
                for u in range(4):
                    split_lo(N_WO + 4 + 4 * b + u, M_WO + 4 + 4 * b + u, j * 2, j * 2)
                for a in range(2):
                    add_square(norm11, 4 * j + 2 * b + a, a, SEQ)
        for u in range(4):
            split_lo(N_WO + 28 + u, M_WO + 28 + u)
        for kt in range(KT - 4, KT):
            add_square(norm11, kt, kt % 2, SEQ)

        prime(N_FFN1, M_FFN1)
        reciprocal_root(norm11, SEQ)
        update(norm11, lambda kt, o, w: Y1[:, kt, o:o + w], 5, latent, CTX, SEQ)
        reciprocal_root(norm12, SEQ)
        apply(norm12, 1, 3, 6, latent, CTX)
        run_ffn(1, N_FFN1, M_FFN1, SEQ, norm13)
        reciprocal_root(norm13, SEQ)
        update(norm13, lambda kt, o, w: Y[:, kt, o:o + w], 7, latent, CTX, SEQ)
        for t in range(2):
            for q in (1, 3):
                dve.wait_ge(out_T, 4 * t + q + 1)
                nc.vector.tensor_copy(OUTT[:, t, 512 * q:512 * q + 512], PS[4 * t + q][:, :]).then_inc(out_b, 1)

    @block.gpsimd
    def _(gp):
        nc.gpsimd.memset(ONES[:, :], 1.0).then_inc(ones_ready, 1)
        nc.gpsimd.memset(SIL[:, :, :], 0.0).then_inc(sil_zero, 1)
        for buf in (PU, PA, PB):
            ins = nc.gpsimd.memset(buf[:, :, :], 0.0)
        ins.then_inc(pool["d"], 1)
        gp.wait_ge(pool["d"], 1)

        width = SEQ + 2 * PAD

        def window_sums(kt, g):
            gp.wait_ge(pool["u"], kt + 1)
            gp.wait_ge(pool["d"], kt + 1)
            lo, hi, src = 0, width, PU
            for step in range(g + 1):
                left, right = (1, 0) if step == 0 else (1 << (step - 1), 1 << (step - 1))
                lo, hi = lo + left, hi - right
                dst = (PA, PB)[step % 2]
                if step:
                    gp.wait_ge(pool["partial"], 2 * g * (g - 1) + (kt - 4 * g) * g + step)
                ins = nc.gpsimd.tensor_tensor(dst[:, :, lo:hi], src[:, :, lo - left:hi - left],
                                              src[:, :, lo + right:hi + right], ALU.add)
                ins.then_inc(pool["s"] if step == g else pool["partial"], 1)
                src = dst

        for g in range(4):
            with gp.Fori(0, 4) as j:
                window_sums(j + 4 * g, g)

        gp.wait_ge(norm01["t"], KT)
        nc.gpsimd.memset(Y[:, :, :], 0.0).then_inc(ffn[0]["y_free"], 4)
        gp.wait_ge(mult_done, M_DQKV + DQKV_U)
        nc.gpsimd.memset(QR[ROPE:P, :, 0, :].bitcast(F32), 0.0).then_inc(hd["qr_zero"], 1)
        nc.gpsimd.memset(QR[0:ROPE, :, 1, :].bitcast(F32), 0.0).then_inc(hd["qr_zero"], 1)
        gp.wait_ge(mult_done, M_WO + 32)
        nc.gpsimd.memset(Y[:, :, 0:SEQ], 0.0).then_inc(ffn[1]["y_free"], 4)

    stack.close()


def shape_constants():
    mats = np.zeros((P, P + 2 + P), np.float32)
    mats[:, 0:P] = np.eye(P)
    for r in range(P):
        if r % 32 < 2:
            mats[r, P + r % 32] = 1.0
        if (r // 16) % 2 == 0:
            mats[r + 16, P + 2 + r] = -1.0
        else:
            mats[r - 16, P + 2 + r] = 1.0
    axis = ROPE // 2
    inv = (np.float32(ROPE_BASE) ** (-np.arange(0, axis, 2, dtype=np.float32) / np.float32(axis))).astype(np.float32)
    t = np.arange(SEQ)
    ang = [(t // GRID_W).astype(np.float32)[None] * inv[:, None], (t % GRID_W).astype(np.float32)[None] * inv[:, None]]
    ang = np.concatenate([ang[0], ang[0], ang[1], ang[1]] * 2)
    rope = np.concatenate([np.cos(ang), np.sin(ang)], axis=1).astype(np.float32)
    counts = [np.minimum(t + w // 2, SEQ) - np.maximum(t - w // 2, 0) for w in WINDOWS]
    inverse = np.tile((1.0 / np.concatenate(counts)).astype(np.float32), (P, 1))
    return {"mats": mats, "rope_tables": rope, "pool_inv": inverse}


_INS = ["x", "ctx", "c", "c_ctx", "ada_w", "ada_b", "norm_g", "pool_w", "pool_scale", "mla_w_dqkv", "mla_q_norm",
        "mla_w_uq", "mla_kv_norm", "mla_w_ukv", "mla_w_o", "ffn_w1", "ffn_w3", "ffn_w2"]


def kernel(**inputs):
    import concourse.bacc as bacc
    from concourse.bass_utils import run_bass_kernel_spmd

    nc = bacc.Bacc("TRN2", target_bir_lowering=False, num_devices=1)
    arrays, args = {}, []
    for name, a in [(k, inputs[k]) for k in _INS] + list(shape_constants().items()):
        arrays["in_" + name] = np.ascontiguousarray(a)
        args.append(nc.dram_tensor("in_" + name, arrays["in_" + name].shape, F32, kind="ExternalInput").ap())
    out = nc.dram_tensor("out", (1, SEQ, D), F32, kind="ExternalOutput").ap()
    program(nc, *args, out)
    return run_bass_kernel_spmd(nc, [arrays], core_ids=[0]).results[0]["out"]
```
